# Optimizing a Trainium2 kernel written in Bass

```python
import jax, jax.numpy as jnp
from jax import lax
import numpy as np

D_MODEL = 1024
BATCH = 1
SEQ = 512
DEPTH = 2

HEAD_DIM = 64
N_ATTN_HEADS = 8
N_IDX_HEADS = 4
IDX_DIM = 64
TOPK_MAX = 256
POOL_WINDOWS = (2, 4, 8, 16)
N_POOL_GROUPS = 4
POOL_GROUP_DIM = 64
N_MEM_HEADS = 4
N_MEM = 256
D_FF = 2816
Q_BLOCK = 128
EPS = 1e-6

ATTN_W = N_ATTN_HEADS * HEAD_DIM
POOL_W = N_POOL_GROUPS * POOL_GROUP_DIM
MEM_W = N_MEM_HEADS * HEAD_DIM
D_MIX = ATTN_W + POOL_W + MEM_W
IN_SIZES = (ATTN_W, ATTN_W, ATTN_W, N_IDX_HEADS * IDX_DIM, IDX_DIM, N_IDX_HEADS, POOL_W, MEM_W)
IN_OFFSETS = tuple(sum(IN_SIZES[:i + 1]) for i in range(len(IN_SIZES) - 1))
D_IN = sum(IN_SIZES)

kernel_name = "hybrid_dsa_pool_memory_macaron"

def rms_norm(x, g):
    xf = x.astype(jnp.float32)
    y = xf * lax.rsqrt(jnp.mean(xf * xf, axis=-1, keepdims=True) + EPS)
    return (y * g.astype(jnp.float32)).astype(x.dtype)

def swiglu(h, w_gate, w_up, w_down):
    return (jax.nn.silu(h @ w_gate) * (h @ w_up)) @ w_down

def dsa_attention(q, k, v, iq, ik, iw):
    B, S = q.shape[0], q.shape[1]
    n_sel = min(TOPK_MAX, S // 4)
    nb = S // Q_BLOCK
    pos = jnp.arange(S, dtype=jnp.int32)

    def to_blocks(a):
        return jnp.moveaxis(a.reshape((B, nb, Q_BLOCK) + a.shape[2:]), 1, 0)

    def block(args):
        qb, iqb, iwb, tb = args
        dots = jnp.einsum('bqhd,bsd->bqhs', iqb, ik).astype(jnp.float32) * (IDX_DIM ** -0.5)
        score = jnp.einsum('bqhs,bqh->bqs', jax.nn.relu(dots),
                           iwb.astype(jnp.float32) * (N_IDX_HEADS ** -0.5))
        score = jnp.where(pos[None, None, :] <= tb[None, :, None], score, -jnp.inf)
        _, idx = lax.top_k(score, n_sel)
        valid = idx <= tb[None, :, None]
        kg = jax.vmap(lambda kb, ib: kb[ib])(k, idx)
        vg = jax.vmap(lambda vb, ib: vb[ib])(v, idx)
        logits = jnp.einsum('bqhd,bqkhd->bhqk', qb, kg).astype(jnp.float32) * (HEAD_DIM ** -0.5)
        logits = jnp.where(valid[:, None], logits, -jnp.inf)
        p = jax.nn.softmax(logits, axis=-1).astype(vg.dtype)
        return jnp.einsum('bhqk,bqkhd->bqhd', p, vg)

    out = lax.map(block, (to_blocks(q), to_blocks(iq), to_blocks(iw), pos.reshape(nb, Q_BLOCK)))
    return jnp.moveaxis(out, 0, 1).reshape(B, S, -1)

def multiscale_pool(u, w_pool, scale):
    B, S = u.shape[0], u.shape[1]
    uf = u.astype(jnp.float32)
    c = jnp.cumsum(uf, axis=1)
    t1 = jnp.arange(1, S + 1, dtype=jnp.float32)
    means = []
    for g, win in enumerate(POOL_WINDOWS):
        cg = c[:, :, g]
        lagged = jnp.pad(cg, ((0, 0), (win, 0), (0, 0)))[:, :S]
        means.append((cg - lagged) / jnp.minimum(t1, float(win))[None, :, None])
    pooled = (jnp.stack(means, axis=2) - uf).astype(u.dtype)
    y = jnp.einsum('bsgc,gcd->bsgd', pooled, w_pool)
    return y.reshape(B, S, POOL_W) * scale

def memory_attention(mq, mem_n, w_kv, mq_g, mk_g):
    B, M = mem_n.shape[0], mem_n.shape[1]
    mk, mv = jnp.split(mem_n @ w_kv, 2, axis=-1)
    mk = rms_norm(mk.reshape(B, M, N_MEM_HEADS, HEAD_DIM), mk_g)
    mv = mv.reshape(B, M, N_MEM_HEADS, HEAD_DIM)
    mq = rms_norm(mq, mq_g)
    logits = jnp.einsum('bshd,bmhd->bhsm', mq, mk).astype(jnp.float32) * (HEAD_DIM ** -0.5)
    p = jax.nn.softmax(logits, axis=-1).astype(mv.dtype)
    out = jnp.einsum('bhsm,bmhd->bshd', p, mv)
    return out.reshape(out.shape[0], out.shape[1], MEM_W)

def setup_inputs(seed: int = 0) -> dict:
    key = jax.random.key(seed)
    ks = jax.random.split(key, 24)
    f32 = jnp.float32

    def nrm(k, shape, fan_in):
        return jax.random.normal(k, shape, f32) * (fan_in ** -0.5)

    def gain(k, shape):
        return 1.0 + 0.02 * jax.random.normal(k, shape, f32)

    return {
        "x": jax.random.normal(ks[0], (BATCH, SEQ, D_MODEL), f32),
        "mem": jax.random.normal(ks[1], (BATCH, N_MEM, D_MODEL), f32),
        "ffn1_norm": gain(ks[2], (DEPTH, D_MODEL)),
        "ffn1_gate": nrm(ks[3], (DEPTH, D_MODEL, D_FF), D_MODEL),
        "ffn1_up": nrm(ks[4], (DEPTH, D_MODEL, D_FF), D_MODEL),
        "ffn1_down": nrm(ks[5], (DEPTH, D_FF, D_MODEL), D_FF),
        "mix_norm": gain(ks[6], (DEPTH, D_MODEL)),
        "mem_norm": gain(ks[7], (DEPTH, D_MODEL)),
        "w_in": nrm(ks[8], (DEPTH, D_MODEL, D_IN), D_MODEL),
        "q_norm": gain(ks[9], (DEPTH, HEAD_DIM)),
        "k_norm": gain(ks[10], (DEPTH, HEAD_DIM)),
        "w_pool": nrm(ks[11], (DEPTH, N_POOL_GROUPS, POOL_GROUP_DIM, POOL_GROUP_DIM), POOL_GROUP_DIM),
        "pool_scale": gain(ks[12], (DEPTH, POOL_W)),
        "w_mem_kv": nrm(ks[13], (DEPTH, D_MODEL, 2 * MEM_W), D_MODEL),
        "mq_norm": gain(ks[14], (DEPTH, HEAD_DIM)),
        "mk_norm": gain(ks[15], (DEPTH, HEAD_DIM)),
        "w_out": nrm(ks[16], (DEPTH, D_MIX, D_MODEL), D_MIX),
        "ffn2_norm": gain(ks[17], (DEPTH, D_MODEL)),
        "ffn2_gate": nrm(ks[18], (DEPTH, D_MODEL, D_FF), D_MODEL),
        "ffn2_up": nrm(ks[19], (DEPTH, D_MODEL, D_FF), D_MODEL),
        "ffn2_down": nrm(ks[20], (DEPTH, D_FF, D_MODEL), D_FF),
    }

def reference(x, mem, ffn1_norm, ffn1_gate, ffn1_up, ffn1_down, mix_norm, mem_norm, w_in,
              q_norm, k_norm, w_pool, pool_scale, w_mem_kv, mq_norm, mk_norm, w_out,
              ffn2_norm, ffn2_gate, ffn2_up, ffn2_down):
    B, S = x.shape[0], x.shape[1]
    for l in range(DEPTH):
        x = x + 0.5 * swiglu(rms_norm(x, ffn1_norm[l]), ffn1_gate[l], ffn1_up[l], ffn1_down[l])

        h = rms_norm(x, mix_norm[l])
        z = h @ w_in[l]
        aq, ak, av, iq, ik, iw, pu, mq = jnp.split(z, IN_OFFSETS, axis=-1)

        aq = rms_norm(aq.reshape(B, S, N_ATTN_HEADS, HEAD_DIM), q_norm[l])
        ak = rms_norm(ak.reshape(B, S, N_ATTN_HEADS, HEAD_DIM), k_norm[l])
        av = av.reshape(B, S, N_ATTN_HEADS, HEAD_DIM)
        iq = iq.reshape(B, S, N_IDX_HEADS, IDX_DIM)
        y_attn = dsa_attention(aq, ak, av, iq, ik, iw)

        y_pool = multiscale_pool(pu.reshape(B, S, N_POOL_GROUPS, POOL_GROUP_DIM),
                                 w_pool[l], pool_scale[l])

        y_mem = memory_attention(mq.reshape(B, S, N_MEM_HEADS, HEAD_DIM),
                                 rms_norm(mem, mem_norm[l]), w_mem_kv[l],
                                 mq_norm[l], mk_norm[l])

        x = x + jnp.concatenate([y_attn, y_pool, y_mem], axis=-1) @ w_out[l]

        x = x + 0.5 * swiglu(rms_norm(x, ffn2_norm[l]), ffn2_gate[l], ffn2_up[l], ffn2_down[l])
    return x


_drawn_inputs = setup_inputs


def setup_inputs(seed=0):
    import zlib

    import numpy as np

    out = dict(_drawn_inputs(seed))
    spreads = {}
    factors = {'ffn1_norm': 3.304,
     'mix_norm': 2.688,
     'mem_norm': 8.0,
     'q_norm': 8.0,
     'k_norm': 8.0,
     'pool_scale': 4.439,
     'mq_norm': 8.0,
     'mk_norm': 8.0,
     'ffn2_norm': 4.679}
    for name, (base, spread) in spreads.items():
        noise = np.random.default_rng([zlib.crc32(name.encode()), seed]).standard_normal(out[name].shape)
        drawn = base * np.exp(spread * noise) if base else spread * noise
        out[name] = __import__('jax').numpy.asarray(drawn.astype(out[name].dtype))
    for name, factor in factors.items():
        out[name] = (out[name] * factor).astype(out[name].dtype)
    return out
```

```python
import concourse.bass as bass
from concourse import mybir

P = 128
D = 1024
T = 512
LAYERS = 2
HD = 64
HEADS = 8
IDX_HEADS = 4
MEM_HEADS = 4
MEM = 256
FF = 2816
TOPK = min(256, T // 4)
WINDOWS = (2, 4, 8, 16)
EPS = 1e-6

DC = D // P
TT = T // P
MT = MEM // P
FC = FF // P
SLOT = DC * P
RING = 4

MIX_SLOTS = (("iq", 2), ("ik", 1), ("iw", 1), ("av", 4), ("aq", 4), ("ak", 4), ("mq", 2), ("pu", 2),
             ("mk", 2), ("mv", 2), ("out", 8))
FFN_SLOTS = 2 * FC + FC
MIX_BASE = {}
_at = FFN_SLOTS
for _name, _n in MIX_SLOTS:
    MIX_BASE[_name] = _at
    _at += _n
FFN_BASE = (0, _at)
SLOTS = _at + FFN_SLOTS
assert SLOTS % RING == 0

G_FFN1, G_MIX, G_FFN2, G_MEM = 0, DC, 2 * DC, 3 * DC
G_Q, G_K, G_MQ, G_MK, G_POOL = (4 * DC + i for i in range(5))
PARAMS = 4 * DC + 4 + 2

NORMED = HEADS // 2 * 2 + MEM_HEADS // 2
NROW = 2 * NORMED
C_ID = 0
C_ONES = C_ID + P
C_BLOCK = C_ONES + P
C_CAUSAL = C_BLOCK + P
C_SEL = C_CAUSAL + T
C_SPREAD = C_SEL + NORMED * NROW
C_INV = C_SPREAD + NORMED * P
C_INVW = C_INV + 2 * 16
C_EPS = C_INVW + 2
CONSTS = C_EPS + 1

NEG = -1e30
TAKEN = -3e38
ROUNDS = TOPK // 8
ROUNDS_PER_STEP = 4
PAD = 16
UNITS_PER_TILE = HEADS + MEM_HEADS
UNITS = TT * UNITS_PER_TILE

DVE_CHAIN = 123


def build(nc, x_t, mem_t, weights, pool_w, params, consts, out):
    f32, f32r = mybir.dt.float32, mybir.dt.float32r
    ALU, ACT = mybir.AluOpType, mybir.ActivationFunctionType
    ds = bass.ds

    base = -(-nc.sbuf_base // 64) * 64
    tile_b = T * 4

    def place(name, cols, at, dt=f32, parts=P):
        return nc.alloc_sbuf_tensor_at(name, [parts, cols], dt, offset=at)

    cursor = [base]

    def new(name, cols, dt=f32, parts=P):
        at = cursor[0]
        cursor[0] += -(-cols * 4 // 64) * 64
        return place(name, cols, at, dt, parts)

    x = new("x", DC * T)
    h_at = cursor[0]
    h_hi = new("h_hi", DC * T, f32r)
    h_lo = new("h_lo", DC * T, f32r)
    raw = new("raw", RING * SLOT)
    w_hi = new("w_hi", RING * SLOT, f32r)
    w_lo = new("w_lo", RING * SLOT, f32r)
    a_hi_at = cursor[0]
    a_hi = new("a_hi", FC * T, f32r)
    a_lo_at = cursor[0]
    a_lo = new("a_lo", FC * T, f32r)
    r = new("r", T)
    t1 = new("t1", 2 * T)
    t2 = new("t2", 2 * T)
    const = new("const", CONSTS)
    par = new("par", LAYERS * PARAMS)
    wpool = new("wpool", 2 * P)
    rmem = new("rmem", MEM)
    cols = new("cols", TT + TT * IDX_HEADS)
    rmem_col = new("rmem_col", MT)
    top8 = new("top8", 8)
    rowmax = new("rowmax", UNITS)
    negmax = new("negmax", UNITS)
    rowsum = new("rowsum", UNITS)
    rinv = new("rinv", UNITS)
    assert cursor[0] <= nc.sbuf_usable_end, cursor[0]
    y_hi, y_lo = a_hi, a_lo
    m_hi = a_hi[:, 8 * T:8 * T + DC * MEM]
    m_lo = a_lo[:, 8 * T:8 * T + DC * MEM]
    z = place("z", NORMED * T, a_hi_at + 12 * tile_b)
    mem = place("mem", DC * MEM, a_hi_at)
    u = place("u", 2 * (PAD + T), a_hi_at + 4 * tile_b)
    wa = place("wa", PAD + T, a_hi_at + 4 * tile_b + 2 * (PAD + T) * 4)
    iq = place("iq", 2 * T, a_lo_at)
    ik = place("ik", T, a_lo_at + 2 * tile_b)
    iw = place("iw", T, a_lo_at + 3 * tile_b)
    wb = place("wb", PAD + T, a_lo_at + 4 * tile_b)
    hrms = place("hrms", T, a_lo_at + 6 * tile_b, parts=NROW)
    v = place("v", TT * T, a_lo_at + 12 * tile_b)
    mk = place("mk", 2 * MEM, a_lo_at + 16 * tile_b)
    mv = place("mv", MT * MEM, a_lo_at + 17 * tile_b)
    score_at = [0, 0, 2 * P, 5 * P]
    score = place("score", 9 * P, a_lo_at + 18 * tile_b)
    mkrms = place("mkrms", 2 * MEM, a_lo_at + 21 * tile_b)
    sq = place("sq", DC * T, a_lo_at + 14 * tile_b)
    pt = place("pt", 2 * T, h_at)
    o_sb = place("o_sb", 2 * T, h_at + 2 * tile_b)

    bank = [nc.alloc_psum_tensor(f"bank{i}", [P, 512], f32) for i in range(8)]

    def chunk(t, j, n=T, size=None):
        return t[:, j * n:j * n + (size or n)]

    def con(at, n=1, parts=P):
        return const[0:parts, at:at + n]

    def sem(name):
        return nc.alloc_semaphore(name)

    w_loaded = [sem(f"w_loaded{i}") for i in range(RING)]
    w_hi_done = sem("w_hi_done")
    w_ready = sem("w_ready")
    slot_done = sem("slot_done")
    acc_done = sem("acc_done")
    setup_loaded = sem("setup_loaded")
    mem_loaded = sem("mem_loaded")
    pool_w_loaded = sem("pool_w_loaded")
    out_stored = sem("out_stored")
    x_new = sem("x_new")
    hi_ready = sem("hi_ready")
    lo_ready = sem("lo_ready")
    sq_ready = sem("sq_ready")
    ssq_ready = sem("ssq_ready")
    sum_done = sem("sum_done")
    rms_ready = sem("rms_ready")
    r_ready = sem("r_ready")
    gate_ready = sem("gate_ready")
    gu_free = sem("gu_free")
    silu_ready = sem("silu_ready")
    prod_ready = sem("prod_ready")
    a_hi_ready = sem("a_hi_ready")
    a_lo_ready = sem("a_lo_ready")
    proj_ready = sem("proj_ready")
    msq_ready = sem("msq_ready")
    mssq_ready = sem("mssq_ready")
    msum_done = sem("msum_done")
    mrms_ready = sem("mrms_ready")
    rmem_ready = sem("rmem_ready")
    m_hi_ready = sem("m_hi_ready")
    m_lo_ready = sem("m_lo_ready")
    cols_done = sem("cols_done")
    cols_ready = sem("cols_ready")
    mcols_done = sem("mcols_done")
    mcols_ready = sem("mcols_ready")
    v_ready = sem("v_ready")
    mv_ready = sem("mv_ready")
    dots_done = sem("dots_done")
    relu_ready = sem("relu_ready")
    acc_score = sem("acc_score")
    bias_ready = sem("bias_ready")
    zsq_ready = sem("zsq_ready")
    zsum_done = sem("zsum_done")
    hrms_ready = sem("hrms_ready")
    hinv_ready = sem("hinv_ready")
    spread_done = sem("spread_done")
    zn_ready = sem("zn_ready")
    pooled_ready = sem("pooled_ready")
    pool_done = sem("pool_done")
    ypool_hi = sem("ypool_hi")
    ypool_lo = sem("ypool_lo")
    logit_done = sem("logit_done")
    lm_ready = sem("lm_ready")
    nm_ready = sem("nm_ready")
    p_ready = sem("p_ready")
    ptp_done = sem("ptp_done")
    pt_ready = sem("pt_ready")
    pv_done = sem("pv_done")
    o_ready = sem("o_ready")
    ot_done = sem("ot_done")
    yt_hi = sem("yt_hi")
    yt_lo = sem("yt_lo")
    dve_chain = sem("dve_chain")

    ACC = 7
    ACC_BASE = (0, FC * ACC, FC * ACC + 8 * ACC)
    ACC_LAYER = ACC * (2 * FC + 8)

    def unit(n):
        i, h = divmod(n, UNITS_PER_TILE)
        is_mem = h >= HEADS
        return i, (h - HEADS if is_mem else h), is_mem, (MT if is_mem else i + 1)

    def group_end(g):
        i, is_mem = divmod(g, 2)
        return i * UNITS_PER_TILE + (UNITS_PER_TILE if is_mem else HEADS)

    group_after = {group_end(g): g for g in range(2 * TT)}

    passed = {"pool": sem("pool_passed"), "dve": sem("dve_passed")}

    def wait_apart(eng, name, s, value):
        eng.wait_ge(s, value)
        eng.sem_inc(passed[name], 1)

    with nc.Block() as block:

        @block.sync
        def _(sp):
            sp.dma_start(x[:, :], x_t[:, :]).then_inc(setup_loaded, 16)
            sp.dma_start(par[:, :], params[:, :]).then_inc(setup_loaded, 16)
            sp.dma_start(const[:, :], consts[:, :]).then_inc(setup_loaded, 16)

            def load(n, first=False):
                for pos in range(RING):
                    if not first:
                        sp.wait_ge(w_ready, n + (pos + 1 - RING))
                    src = weights[ds(n + pos, 1), :, :].rearrange("a p n -> (a p) n")
                    sp.dma_start(raw[:, pos * SLOT:(pos + 1) * SLOT], src).then_inc(w_loaded[pos], 16)

            load(0, first=True)
            with sp.Fori(1, LAYERS * SLOTS // RING) as i:
                load(i * RING)
            for j in range(DC):
                sp.wait_ge(x_new, DC + 3 * DC * LAYERS - DC + j + 1)
                sp.dma_start(out[:, j * T:(j + 1) * T], chunk(x, j)).then_inc(out_stored, 16)
            sp.wait_ge(out_stored, 16 * DC)

        @block.gpsimd
        def _(pool):
            def split(n, turn, first=False):
                for pos in range(RING):
                    s = slice(pos * SLOT, (pos + 1) * SLOT)
                    if not first:
                        pool.wait_ge(slot_done, n + (pos + 1 - RING))
                    wait_apart(pool, "pool", w_loaded[pos], (turn + 1) * 16)
                    nc.gpsimd.tensor_copy(w_hi[:, s], raw[:, s]).then_inc(w_hi_done, 1)
                    pool.wait_ge(w_hi_done, n + (pos + 1))
                    nc.gpsimd.tensor_tensor(out=w_lo[:, s], in0=raw[:, s], in1=w_hi[:, s].bitcast(f32),
                                            op=ALU.subtract).then_inc(w_ready, 1)

            split(0, 0, first=True)
            with pool.Fori(1, LAYERS * SLOTS // RING) as i:
                split(i * RING, i)

        @block.tensor
        def _(pe):
            def mm(out_, lhsT, rhs, start=True, stop=True):
                return nc.tensor.matmul(out_, lhsT, rhs, start=start, stop=stop, skip_group_check=True)

            def passes(out_, w, act, start, stop):
                (whi, wlo), (ahi, alo) = w, act
                mm(out_, whi, ahi, start, False)
                mm(out_, whi, alo, False, False)
                return mm(out_, wlo, ahi, False, stop)

            def weight(pos, at, n=P):
                s = slice(pos * SLOT + at, pos * SLOT + at + n)
                return w_hi[:, s], w_lo[:, s]

            def pair(hi, lo, at, n=T):
                return hi[:, at:at + n], lo[:, at:at + n]

            def project(l, n, to, hi, lo, width=T, lo_sem=None):
                pe.wait_ge(w_ready, l * SLOTS + (n + 1))
                for k in range(DC):
                    if lo_sem is not None:
                        pe.wait_ge(lo_ready, lo_sem + (k + 1))
                    last = passes(to, weight(n % RING, k * P), pair(hi, lo, k * width, width),
                                  k == 0, k == DC - 1)
                last.then_inc(slot_done, 1)

            def token_sums(l, ph):
                pe.wait_ge(ssq_ready, l * 3 + (ph + 1))
                mm(bank[4][:, :], con(C_ONES, P), chunk(sq, 0)).then_inc(sum_done, 1)

            def accumulate(pos, hi, lo, start, stop):
                for j in range(DC):
                    last = passes(bank[j][:, :], weight(pos, j * P), (hi, lo), start, stop)
                    if j < ACC:
                        last.then_inc(acc_done, 1)
                    else:
                        last.then_inc(slot_done, 1)

            def ffn(l, e):
                ph, ffn_at = 2 * e, FFN_BASE[e]
                def gate_up(f, half, first=False):
                    n = ffn_at + 2 * half
                    pe.wait_ge(gu_free, (l * 2 + e) * FC + (f + (half + 1)))
                    at = l * SLOTS + ffn_at + f * 2 + 2 * half
                    for up in range(2):
                        pos = (n + up) % RING
                        pe.wait_ge(w_ready, at + (up + 1))
                        for k in range(DC):
                            if first and half == 0 and up == 0:
                                pe.wait_ge(lo_ready, (l * 3 + ph) * DC + (k + 1))
                            last = passes(bank[2 * half + up][:, :], weight(pos, k * P),
                                          pair(h_hi, h_lo, k * T), k == 0, k == DC - 1)
                        last.then_inc(slot_done, 1)
                        if first and half == 0 and up == 0:
                            token_sums(l, ph)

                gate_up(0, 0, first=True)
                gate_up(0, 1)
                with pe.Fori(1, FC // 2) as i:
                    gate_up(i * 2, 0)
                    gate_up(i * 2, 1)

                down_at = ffn_at + 2 * FC
                def down(f, off, start=False, stop=False):
                    at = l * SLOTS + down_at + f + off
                    pe.wait_ge(w_ready, at + 1)
                    pe.wait_ge(a_lo_ready, (l * 2 + e) * FC + (f + (off + 1)))
                    fo = f * T + off * T
                    pos = (down_at + off + (f if isinstance(f, int) else 0)) % RING
                    accumulate(pos, a_hi[:, ds(fo, T)], a_lo[:, ds(fo, T)], start, stop)

                pe.wait_ge(rms_ready, l * 3 + (ph + 1))
                pe.wait_ge(gu_free, (l * 2 + e) * FC + (FC + 2))
                down(0, 0, start=True)
                down(0, 1)
                with pe.Fori(0, (FC - 2) // RING - 1) as i:
                    for off in range(RING):
                        down(i * RING, 2 + off)
                for off in range(RING):
                    down(FC - RING, off, stop=off == RING - 1)

            def mix(l):
                def at(name, i=0):
                    return MIX_BASE[name] + i

                def heads_sum(j):
                    pe.wait_ge(zsq_ready, l * (NORMED + 1) + (j + 1))
                    mm(bank[6][0:NROW, :], con(C_SEL + j * NROW, NROW), chunk(t1, j % 2),
                       j == 0, j == NORMED - 1).then_inc(zsum_done, 1)

                project(l, at("iq", 0), bank[0][:, :], h_hi, h_lo, lo_sem=(l * 3 + 1) * DC)
                token_sums(l, 1)
                project(l, at("iq", 1), bank[1][:, :], h_hi, h_lo)
                project(l, at("ik"), bank[2][:, :], h_hi, h_lo)
                project(l, at("iw"), bank[3][:, :], h_hi, h_lo)
                pe.wait_ge(rms_ready, l * 3 + 2)
                for s in range(4):
                    n = at("av", s)
                    pe.wait_ge(w_ready, l * SLOTS + (n + 1))
                    for half in range(2):
                        k = 2 * s + half
                        whi, wlo = weight(n % RING, half * T, T)
                        for i in range(TT):
                            hhi, hlo = pair(h_hi, h_lo, k * T + i * P, P)
                            last = passes(bank[4 + i][:, :], (hhi, hlo), (whi, wlo),
                                          k == 0, k == DC - 1)
                    last.then_inc(slot_done, 1)
                pe.wait_ge(proj_ready, l * 17 + 4)
                for i in range(TT):
                    mm(bank[3][:, i:i + 1], r[0:1, i * P:(i + 1) * P], con(C_ONES, 1, 1))
                for i in range(TT):
                    last = mm(bank[3][:, TT + 4 * i:TT + 4 * i + 4], iw[0:4, i * P:(i + 1) * P],
                              con(C_ID, 4, 4))
                last.then_inc(cols_done, 1)
                pe.wait_ge(mssq_ready, l + 1)
                mm(bank[2][:, 0:MEM], con(C_ONES, P), sq[:, 0:MEM]).then_inc(msum_done, 1)
                n = 0
                for i in range(1, TT):
                    for h in range(IDX_HEADS):
                        if n >= 2:
                            pe.wait_ge(relu_ready, l * 12 + (n - 1))
                        p0 = HD * (h % 2)
                        mm(bank[n % 2][:, 0:(i + 1) * P],
                           iq[p0:p0 + HD, (h // 2) * T + i * P:(h // 2) * T + (i + 1) * P],
                           ik[p0:p0 + HD, 0:(i + 1) * P]).then_inc(dots_done, 1)
                        n += 1
                pe.wait_ge(rmem_ready, l + 1)
                pe.wait_ge(v_ready, (l + 1) * TT)
                for i in range(MT):
                    last = mm(bank[7][:, i:i + 1], rmem[0:1, i * P:(i + 1) * P], con(C_ONES, 1, 1))
                last.then_inc(mcols_done, 1)
                names = [("aq", i) for i in range(4)] + [("ak", i) for i in range(4)] + \
                        [("mq", i) for i in range(2)] + [("pu", i) for i in range(2)]
                for j, (name, i) in enumerate(names):
                    t = j + 4
                    if j < 2:
                        pe.wait_ge(relu_ready, (l + 1) * 12)
                    elif j == 2:
                        pe.wait_ge(mrms_ready, l + 1)
                    elif j == 3:
                        pe.wait_ge(cols_ready, l + 1)
                    else:
                        pe.wait_ge(proj_ready, l * 17 + (t - 3))
                    project(l, at(name, i), bank[t % 4][:, :], h_hi, h_lo)
                    if 0 <= j - 2 < NORMED:
                        heads_sum(j - 2)
                pe.wait_ge(m_lo_ready, l + 1)
                for i in range(2):
                    project(l, at("mk", i), bank[4][:, i * MEM:(i + 1) * MEM], m_hi, m_lo, MEM)
                for s in range(2):
                    n = at("mv", s)
                    pe.wait_ge(w_ready, l * SLOTS + (n + 1))
                    for i in range(MT):
                        if i == 1 and s == 0:
                            pe.wait_ge(proj_ready, l * 17 + 16)
                        for q in range(4):
                            k = 4 * s + q
                            last = passes(bank[5 if i == 0 else 3][:, 0:MEM],
                                          pair(m_hi, m_lo, k * MEM + i * P, P),
                                          weight(n % RING, q * MEM, MEM), k == 0, k == DC - 1)
                    last.then_inc(slot_done, 1)
                pe.wait_ge(zsq_ready, (l + 1) * (NORMED + 1))
                pe.wait_ge(mcols_ready, l + 1)
                mm(bank[7][:, :], con(C_BLOCK, P), chunk(t1, NORMED % 2)).then_inc(zsum_done, 1)
                pe.wait_ge(hinv_ready, l * 2 + 1)
                for j in range(NORMED):
                    if j < 3:
                        pe.wait_ge(proj_ready, l * 17 + (13 + j))
                    else:
                        pe.wait_ge(zn_ready, l * (NORMED + 1) + (j - 2))
                    mm(bank[j % 3][:, :], con(C_SPREAD + j * P, P, NROW), hrms[:, :])\
                        .then_inc(spread_done, 1)
                pe.wait_ge(pool_w_loaded, (l + 1) * 16)
                pe.wait_ge(pooled_ready, (l + 1) * 2)
                pe.wait_ge(hrms_ready, (l + 1) * 2)
                for i in range(2):
                    mm(bank[6 + i][:, :], chunk(wpool, i, P),
                       u[:, i * (PAD + T) + PAD:(i + 1) * (PAD + T)]).then_inc(pool_done, 1)

                pe.wait_ge(zn_ready, (l + 1) * (NORMED + 1))
                pe.wait_ge(mv_ready, (l + 1) * MT)

                def logits(n):
                    i, h, is_mem, blocks = unit(n)
                    if n >= 2:
                        pe.wait_ge(lm_ready, l * UNITS + (n - 1))
                    p0, j = HD * (h % 2), h // 2
                    if is_mem:
                        qt, kt = HEADS + j, mk[p0:p0 + HD, j * MEM:(j + 1) * MEM]
                    else:
                        qt, kt = j, z[p0:p0 + HD, (4 + j) * T:(4 + j) * T + blocks * P]
                    mm(bank[n % 2][:, 0:blocks * P],
                       z[p0:p0 + HD, qt * T + i * P:qt * T + (i + 1) * P], kt).then_inc(logit_done, 1)

                def transpose_p(n):
                    i, h, is_mem, blocks = unit(n)
                    pe.wait_ge(p_ready, l * UNITS + (n + 1))
                    if n >= 2:
                        pe.wait_ge(pt_ready, l * UNITS + (n - 1))
                    for b in range(blocks):
                        last = nc.tensor.transpose(bank[2 + n % 2][:, b * P:(b + 1) * P],
                                                   t1[:, (n % 2) * T + b * P:(n % 2) * T + (b + 1) * P],
                                                   con(C_ID, P))
                    last.then_inc(ptp_done, 1)

                def times_v(n):
                    i, h, is_mem, blocks = unit(n)
                    pe.wait_ge(pt_ready, l * UNITS + (n + 1))
                    if h == 0 and i > 0:
                        pe.wait_ge(o_ready, l * 2 * TT + (2 * i - 1 + is_mem))
                    for b in range(blocks):
                        val = mv[:, b * MEM + h * HD:b * MEM + (h + 1) * HD] if is_mem else \
                            v[:, b * T + h * HD:b * T + (h + 1) * HD]
                        last = mm(bank[4 + is_mem][:, h * HD:(h + 1) * HD],
                                  pt[:, (n % 2) * T + b * P:(n % 2) * T + (b + 1) * P], val,
                                  b == 0, b == blocks - 1)
                    last.then_inc(pv_done, 1)

                def transpose_o(g):
                    i, is_mem = divmod(g, 2)
                    pe.wait_ge(o_ready, l * 2 * TT + (g + 1))
                    if g >= 2:
                        pe.wait_ge(yt_lo, l * 2 * TT + (g - 1))
                    else:
                        pe.wait_ge(ypool_lo, (l + 1) * 2)
                    for b in range(2 if is_mem else 4):
                        last = nc.tensor.transpose(bank[6 + is_mem][:, b * P:(b + 1) * P],
                                                   o_sb[:, is_mem * T + b * P:is_mem * T + (b + 1) * P],
                                                   con(C_ID, P))
                    last.then_inc(ot_done, 1)

                for n in range(UNITS + 3):
                    if n < UNITS:
                        logits(n)
                    if 0 <= n - 1 < UNITS:
                        transpose_p(n - 1)
                    if 0 <= n - 2 < UNITS:
                        times_v(n - 2)
                    if n - 3 + 1 in group_after:
                        transpose_o(group_after[n - 3 + 1])

                pe.wait_ge(yt_lo, (l + 1) * 2 * TT)
                for k in range(DC):
                    n = at("out", k)
                    pe.wait_ge(w_ready, l * SLOTS + (n + 1))
                    accumulate(n % RING, chunk(y_hi, k), chunk(y_lo, k), k == 0, k == DC - 1)

            pe.wait_ge(setup_loaded, 48)
            with pe.Fori(0, LAYERS) as l:
                ffn(l, 0)
                mix(l)
                ffn(l, 1)

        @block.scalar
        def _(act):
            def prepare(l, ph, gain):
                for j in range(DC):
                    act.wait_ge(x_new, (l * 3 + ph) * DC + (j + 1))
                    nc.scalar.activation(chunk(h_hi, j), chunk(x, j), ACT.Copy,
                                         scale=par[:, ds(l * PARAMS + (gain + j), 1)])\
                        .then_inc(hi_ready, 1)
                for half in range(2):
                    s = slice(half * 4 * T, (half + 1) * 4 * T)
                    nc.scalar.activation(sq[:, s], x[:, s], ACT.Square).then_inc(sq_ready, 1)

            def root(l, ph):
                act.wait_ge(sum_done, l * 3 + (ph + 1))
                nc.scalar.activation(r[:, :], bank[4][:, :], ACT.Sqrt, bias=con(C_EPS),
                                     scale=1.0 / D).then_inc(rms_ready, 1)

            def ffn(l, e):
                prepare(l, 2 * e, (G_FFN1, G_FFN2)[e])
                root(l, 2 * e)
                with act.Fori(0, FC // 2) as i:
                    f = i * 2
                    for half in range(2):
                        done = (l * 2 + e) * FC + f + (half + 1)
                        g = chunk(t1, half)
                        act.wait_ge(gate_ready, done)
                        nc.scalar.activation(g, g, ACT.Silu).then_inc(silu_ready, 1)
                        act.wait_ge(prod_ready, done)
                        nc.scalar.activation(a_hi[:, ds(f * T + half * T, T)], chunk(t2, half),
                                             ACT.Copy).then_inc(a_hi_ready, 1)

            def mix(l):
                prepare(l, 1, G_MIX)
                act.dma_start(mem[:, :], mem_t[:, :]).then_inc(mem_loaded, 16)
                act.dma_start(wpool[:, :], pool_w[ds(l, 1), :, :].rearrange("a p n -> (a p) n"))\
                    .then_inc(pool_w_loaded, 16)
                root(l, 1)
                act.wait_ge(mem_loaded, (l + 1) * 16)
                for j in range(DC):
                    s = slice(j * MEM, (j + 1) * MEM)
                    nc.scalar.activation(m_hi[:, s], mem[:, s], ACT.Copy,
                                         scale=par[:, ds(l * PARAMS + (G_MEM + j), 1)])\
                        .then_inc(m_hi_ready, 1)
                nc.scalar.activation(sq[:, 0:DC * MEM], mem[:, :], ACT.Square).then_inc(msq_ready, 1)
                act.wait_ge(msum_done, l + 1)
                nc.scalar.activation(rmem[:, :], bank[2][:, 0:MEM], ACT.Sqrt, bias=con(C_EPS),
                                     scale=1.0 / D).then_inc(mrms_ready, 1)
                act.wait_ge(cols_ready, l + 1)
                act.wait_ge(slot_done, l * SLOTS + (MIX_BASE["av"] + 4))
                for i in range(TT):
                    nc.scalar.activation(chunk(v, i), bank[4 + i][:, :], ACT.Copy,
                                         scale=cols[:, i:i + 1]).then_inc(v_ready, 1)
                n = 0
                for i in range(1, TT):
                    for h in range(IDX_HEADS):
                        act.wait_ge(dots_done, l * 12 + (n + 1))
                        if n >= 2:
                            act.wait_ge(acc_score, l * 12 + (n - 1))
                        nc.scalar.activation(chunk(t2, n % 2, T, (i + 1) * P), bank[n % 2][:, 0:(i + 1) * P],
                                             ACT.Relu, scale=HD ** -0.5 * IDX_HEADS ** -0.5)\
                            .then_inc(relu_ready, 1)
                        n += 1
                for j in range(NORMED):
                    act.wait_ge(proj_ready, l * 17 + (5 + j))
                    if j >= 2:
                        act.wait_ge(zsum_done, l * (NORMED + 1) + (j - 1))
                    nc.scalar.activation(chunk(t1, j % 2), chunk(z, j), ACT.Square).then_inc(zsq_ready, 1)
                act.wait_ge(zsum_done, l * (NORMED + 1) + NORMED)
                nc.scalar.activation(hrms[:, :], bank[6][0:NROW, :], ACT.Sqrt, bias=con(C_EPS, 1, NROW),
                                     scale=1.0 / HD).then_inc(hrms_ready, 1)
                act.wait_ge(proj_ready, (l + 1) * 17)
                nc.scalar.activation(chunk(t1, NORMED % 2), mk[:, :], ACT.Square).then_inc(zsq_ready, 1)
                act.wait_ge(slot_done, l * SLOTS + (MIX_BASE["mv"] + 2))
                act.wait_ge(mcols_ready, l + 1)
                for i in range(MT):
                    nc.scalar.activation(chunk(mv, i, MEM), bank[5 if i == 0 else 3][:, 0:MEM], ACT.Copy,
                                         scale=rmem_col[:, i:i + 1]).then_inc(mv_ready, 1)
                act.wait_ge(zsum_done, (l + 1) * (NORMED + 1))
                nc.scalar.activation(mkrms[:, :], bank[7][:, :], ACT.Sqrt, bias=con(C_EPS),
                                     scale=1.0 / HD).then_inc(hrms_ready, 1)
                for i in range(2):
                    act.wait_ge(pool_done, l * 2 + (i + 1))
                    if i == 0:
                        act.wait_ge(pool_done, (l + 1) * 2)
                    nc.scalar.activation(chunk(y_hi, 4 + i), bank[6 + i][:, :], ACT.Copy,
                                         scale=par[:, ds(l * PARAMS + (G_POOL + i), 1)])\
                        .then_inc(ypool_hi, 1)

                def exps(n):
                    i, h, is_mem, blocks = unit(n)
                    act.wait_ge(nm_ready, l * UNITS + (n + 1))
                    if n >= 2:
                        act.wait_ge(ptp_done, l * UNITS + (n - 1))
                    nc.scalar.activation(chunk(t1, n % 2, T, blocks * P), chunk(t2, n % 2, T, blocks * P),
                                         ACT.Exp, bias=negmax[:, n:n + 1], scale=HD ** -0.5,
                                         accum_out=rowsum[:, n:n + 1]).then_inc(p_ready, 1)

                def copy_pt(n):
                    blocks = unit(n)[3]
                    act.wait_ge(ptp_done, l * UNITS + (n + 1))
                    if n >= 2:
                        act.wait_ge(pv_done, l * UNITS + (n - 1))
                    nc.scalar.activation(chunk(pt, n % 2, T, blocks * P), bank[2 + n % 2][:, 0:blocks * P],
                                         ACT.Copy).then_inc(pt_ready, 1)

                def split_y(g):
                    i, is_mem = divmod(g, 2)
                    n = 2 if is_mem else 4
                    y = y_hi[:, (6 if is_mem else 0) * T:(8 if is_mem else 4) * T]
                    act.wait_ge(ot_done, l * 2 * TT + (g + 1))
                    nc.scalar.activation(y.rearrange("p (c t) -> p c t", t=T)[:, :, i * P:(i + 1) * P],
                                         bank[6 + is_mem][:, 0:n * P].rearrange("p (c t) -> p c t", t=P),
                                         ACT.Copy).then_inc(yt_hi, 1)

                for n in range(UNITS + 4):
                    if n < UNITS:
                        exps(n)
                    if 0 <= n - 1 < UNITS:
                        copy_pt(n - 1)
                    if n - 4 + 1 in group_after:
                        split_y(group_after[n - 4 + 1])

            act.wait_ge(setup_loaded, 48)
            with act.Fori(0, LAYERS) as l:
                ffn(l, 0)
                mix(l)
                ffn(l, 1)

        @block.vector
        def _(dve):
            V = nc.vector
            links = [0]

            def link(l, ins):
                links[0] += 1
                ins.then_inc(dve_chain, 1)
                dve.wait_ge(dve_chain, l * DVE_CHAIN + links[0])

            def prepare(l, ph, gain):
                for j in range(DC):
                    dve.wait_ge(hi_ready, (l * 3 + ph) * DC + (j + 1))
                    V.scalar_tensor_tensor(out=chunk(h_lo, j), in0=chunk(x, j),
                                           scalar=par[:, ds(l * PARAMS + (gain + j), 1)],
                                           in1=chunk(h_hi, j).bitcast(f32), op0=ALU.mult,
                                           op1=ALU.subtract).then_inc(lo_ready, 1)
                dve.wait_ge(sq_ready, (l * 3 + ph) * 2 + 2)
                for half in (4 * T, 2 * T):
                    link(l, V.tensor_tensor(out=sq[:, 0:half], in0=sq[:, 0:half],
                                            in1=sq[:, half:2 * half], op=ALU.add))
                V.tensor_tensor(out=sq[:, 0:T], in0=sq[:, 0:T], in1=sq[:, T:2 * T],
                                op=ALU.add).then_inc(ssq_ready, 1)

            def invert(l, ph):
                dve.wait_ge(rms_ready, l * 3 + (ph + 1))
                V.reciprocal(r[:, :], r[:, :]).then_inc(r_ready, 1)
                wait_apart(dve, "dve", r_ready, l * 3 + (ph + 1))

            def update(l, ph, acc_at, slot_at, scale):
                for j in range(DC):
                    if j < ACC:
                        dve.wait_ge(acc_done, l * ACC_LAYER + (acc_at + j + 1))
                    else:
                        dve.wait_ge(slot_done, l * SLOTS + slot_at)
                    V.scalar_tensor_tensor(out=chunk(x, j), in0=bank[j][:, :], scalar=scale,
                                           in1=chunk(x, j), op0=ALU.mult, op1=ALU.add)\
                        .then_inc(x_new, 1)

            def ffn(l, e):
                ph = 2 * e
                prepare(l, ph, (G_FFN1, G_FFN2)[e])
                invert(l, ph)
                with dve.Fori(0, FC // 2) as i:
                    f = i * 2
                    for half in range(2):
                        done = (l * 2 + e) * FC + f + (half + 1)
                        slot = l * SLOTS + FFN_BASE[e] + f * 2 + 2 * half
                        g, h = chunk(t1, half), chunk(t2, half)
                        dve.wait_ge(slot_done, slot + 1)
                        V.tensor_tensor(out=g, in0=bank[2 * half][:, :], in1=r[:, :],
                                        op=ALU.mult).then_inc(gate_ready, 1)
                        dve.wait_ge(slot_done, slot + 2)
                        V.tensor_tensor(out=h, in0=bank[2 * half + 1][:, :], in1=r[:, :],
                                        op=ALU.mult).then_inc(gu_free, 1)
                        dve.wait_ge(gu_free, done + 2)
                        dve.wait_ge(silu_ready, done)
                        V.tensor_tensor(out=h, in0=g, in1=h, op=ALU.mult).then_inc(prod_ready, 1)
                        dve.wait_ge(a_hi_ready, done)
                        V.tensor_tensor(out=a_lo[:, ds(f * T + half * T, T)], in0=h,
                                        in1=a_hi[:, ds(f * T + half * T, T)].bitcast(f32),
                                        op=ALU.subtract).then_inc(a_lo_ready, 1)
                update(l, ph, ACC_BASE[2 * e] + ACC * (FC - 1), FFN_BASE[e] + FFN_SLOTS, 0.5)

            def mix(l):
                prepare(l, 1, G_MIX)
                invert(l, 1)

                for t in (u[:, 0:PAD], u[:, PAD + T:2 * PAD + T], wa[:, 0:PAD]):
                    V.memset(t, 0.0)
                link(l, V.memset(wb[:, 0:PAD], 0.0))

                def evacuate(j, slot, out_, in_, rr):
                    dve.wait_ge(slot_done, l * SLOTS + slot + 1)
                    V.tensor_tensor(out=out_, in0=in_, in1=rr, op=ALU.mult).then_inc(proj_ready, 1)

                evacuate(0, MIX_BASE["iq"], chunk(iq, 0), bank[0][:, :], r[:, :])
                evacuate(1, MIX_BASE["iq"] + 1, chunk(iq, 1), bank[1][:, :], r[:, :])
                evacuate(2, MIX_BASE["ik"], ik[:, :], bank[2][:, :], r[:, :])
                evacuate(3, MIX_BASE["iw"], iw[0:4, :], bank[3][0:4, :], r[0:4, :])
                dve.wait_ge(msq_ready, l + 1)
                for half in (4 * MEM, 2 * MEM):
                    link(l, V.tensor_tensor(out=sq[:, 0:half], in0=sq[:, 0:half],
                                            in1=sq[:, half:2 * half], op=ALU.add))
                V.tensor_tensor(out=sq[:, 0:MEM], in0=sq[:, 0:MEM], in1=sq[:, MEM:2 * MEM],
                                op=ALU.add).then_inc(mssq_ready, 1)
                dve.wait_ge(m_hi_ready, (l + 1) * DC)
                for j in range(DC):
                    s = slice(j * MEM, (j + 1) * MEM)
                    last = V.scalar_tensor_tensor(out=m_lo[:, s], in0=mem[:, s],
                                                  scalar=par[:, ds(l * PARAMS + (G_MEM + j), 1)],
                                                  in1=m_hi[:, s].bitcast(f32), op0=ALU.mult,
                                                  op1=ALU.subtract)
                last.then_inc(m_lo_ready, 1)
                dve.wait_ge(cols_done, l + 1)
                V.tensor_copy(cols[:, :], bank[3][:, 0:TT + 4 * TT]).then_inc(cols_ready, 1)
                dve.wait_ge(cols_ready, l + 1)
                dve.wait_ge(mrms_ready, l + 1)
                V.reciprocal(rmem[:, :], rmem[:, :]).then_inc(rmem_ready, 1)

                n = 0
                for i in range(1, TT):
                    s = score[:, score_at[i]:score_at[i] + (i + 1) * P]
                    for h in range(IDX_HEADS):
                        dve.wait_ge(relu_ready, l * 12 + (n + 1))
                        c = TT + 4 * i + h
                        before = con(C_CAUSAL + T - (i + 1) * P, (i + 1) * P) if h == 0 else s
                        V.scalar_tensor_tensor(out=s, in0=chunk(t2, n % 2, T, (i + 1) * P),
                                               scalar=cols[:, c:c + 1], in1=before, op0=ALU.mult,
                                               op1=ALU.add).then_inc(acc_score, 1)
                        n += 1
                        dve.wait_ge(acc_score, l * 12 + n)
                dve.wait_ge(mcols_done, l + 1)
                V.tensor_copy(rmem_col[:, :], bank[7][:, 0:MT]).then_inc(mcols_ready, 1)

                def take_largest(i):
                    s = score[:, score_at[i]:score_at[i] + (i + 1) * P]
                    start = links[0]
                    with dve.Fori(0, ROUNDS_PER_STEP) as q:
                        now = l * DVE_CHAIN + q * 2 + start
                        V.max(top8[:, :], s).then_inc(dve_chain, 1)
                        wait_apart(dve, "dve", dve_chain, now + 1)
                        V.match_replace(s, top8[:, :], s, TAKEN).then_inc(dve_chain, 1)
                        dve.wait_ge(dve_chain, now + 2)
                    links[0] += 2 * ROUNDS_PER_STEP

                steps = [i for i in range(1, TT) for _ in range(ROUNDS // ROUNDS_PER_STEP)]
                assert len(steps) == NORMED + 2
                for j in range(NORMED + 2):
                    take_largest(steps[j])
                    name = ("aq", "ak", "mq", "pu")[min(j // 4, 2) + (j >= NORMED)]
                    out_ = chunk(z, j) if j < NORMED else \
                        u[:, (j - NORMED) * (PAD + T) + PAD:(j - NORMED + 1) * (PAD + T)]
                    evacuate(4 + j, MIX_BASE["aq"] + j, out_, bank[j % 4][:, :], r[:, :])
                dve.wait_ge(proj_ready, l * 17 + 16)
                V.tensor_scalar(score[:, :], score[:, :], TAKEN, NEG, ALU.not_equal,
                                ALU.mult).then_inc(bias_ready, 1)
                dve.wait_ge(slot_done, l * SLOTS + (MIX_BASE["mk"] + 2))
                for i in range(2):
                    last = V.tensor_tensor(out=mk[:, i * MEM:(i + 1) * MEM],
                                           in0=bank[4][:, i * MEM:(i + 1) * MEM],
                                           in1=rmem[:, :], op=ALU.mult)
                last.then_inc(proj_ready, 1)
                dve.wait_ge(hrms_ready, l * 2 + 1)
                V.reciprocal(hrms[:, :], hrms[:, :]).then_inc(hinv_ready, 1)

                for i in range(2):
                    ui = u[:, i * (PAD + T):(i + 1) * (PAD + T)]
                    def shifted_sum(p0, dst, src, by):
                        link(l, V.tensor_tensor(out=dst[p0:P, PAD:PAD + T], in0=src[p0:P, PAD:PAD + T],
                                                in1=src[p0:P, PAD - by:PAD + T - by], op=ALU.add))
                    if i == 0:
                        shifted_sum(0, wa, ui, 1)
                        shifted_sum(HD, wb, wa, 2)
                        halves = (wa, wb)
                    else:
                        shifted_sum(0, wa, ui, 1)
                        shifted_sum(0, wb, wa, 2)
                        shifted_sum(0, wa, wb, 4)
                        shifted_sum(HD, wb, wa, 8)
                        halves = (wa, wb)
                    for half, w in enumerate(halves):
                        p = slice(half * HD, (half + 1) * HD)
                        link(l, V.tensor_tensor(out=w[p, PAD:PAD + 16], in0=w[p, PAD:PAD + 16],
                                                in1=const[p, C_INV + 16 * i:C_INV + 16 * (i + 1)],
                                                op=ALU.mult))
                        V.scalar_tensor_tensor(out=ui[p, PAD + 16:PAD + T], in0=w[p, PAD + 16:PAD + T],
                                               scalar=const[p, C_INVW + i:C_INVW + i + 1],
                                               in1=ui[p, PAD + 16:PAD + T], op0=ALU.mult,
                                               op1=ALU.subtract)
                        last = V.tensor_tensor(out=ui[p, PAD:PAD + 16], in0=w[p, PAD:PAD + 16],
                                               in1=ui[p, PAD:PAD + 16], op=ALU.subtract)
                    last.then_inc(pooled_ready, 1)
                    dve.wait_ge(pooled_ready, l * 2 + (i + 1))

                gains = [G_Q] * 4 + [G_K] * 4 + [G_MQ] * 2
                for j in range(NORMED):
                    dve.wait_ge(spread_done, l * NORMED + (j + 1))
                    V.scalar_tensor_tensor(out=chunk(z, j), in0=chunk(z, j),
                                           scalar=par[:, ds(l * PARAMS + gains[j], 1)],
                                           in1=bank[j % 3][:, :], op0=ALU.mult,
                                           op1=ALU.mult).then_inc(zn_ready, 1)
                dve.wait_ge(hrms_ready, (l + 1) * 2)
                V.reciprocal(mkrms[:, :], mkrms[:, :]).then_inc(hinv_ready, 1)
                dve.wait_ge(hinv_ready, (l + 1) * 2)
                V.scalar_tensor_tensor(out=mk[:, :], in0=mk[:, :],
                                       scalar=par[:, ds(l * PARAMS + G_MK, 1)],
                                       in1=mkrms[:, :], op0=ALU.mult, op1=ALU.mult)\
                    .then_inc(zn_ready, 1)
                for i in range(2):
                    dve.wait_ge(ypool_hi, l * 2 + (i + 1))
                    V.scalar_tensor_tensor(out=chunk(y_lo, 4 + i), in0=bank[6 + i][:, :],
                                           scalar=par[:, ds(l * PARAMS + (G_POOL + i), 1)],
                                           in1=chunk(y_hi, 4 + i).bitcast(f32), op0=ALU.mult,
                                           op1=ALU.subtract).then_inc(ypool_lo, 1)

                def mask_and_max(n):
                    i, h, is_mem, blocks = unit(n)
                    if is_mem:
                        bias = con(C_CAUSAL, MEM)
                    elif i == 0:
                        bias = con(C_CAUSAL + T - P, P)
                    else:
                        bias = score[:, score_at[i]:score_at[i] + blocks * P]
                    if n >= 2:
                        dve.wait_ge(p_ready, l * UNITS + (n - 1))
                    wait_apart(dve, "dve", logit_done, l * UNITS + (n + 1))
                    V.tensor_tensor_reduce(out=chunk(t2, n % 2, T, blocks * P),
                                           in0=bank[n % 2][:, 0:blocks * P], in1=bias, scale=1.0,
                                           scalar=TAKEN, op0=ALU.add, op1=ALU.max,
                                           accum_out=rowmax[:, n:n + 1]).then_inc(lm_ready, 1)
                    dve.wait_ge(lm_ready, l * UNITS + (n + 1))
                    V.tensor_scalar(negmax[:, n:n + 1], rowmax[:, n:n + 1], -HD ** -0.5, None,
                                    ALU.mult).then_inc(nm_ready, 1)

                def finish(g):
                    i, is_mem = divmod(g, 2)
                    end = group_end(g)
                    n = MEM_HEADS if is_mem else HEADS
                    dve.wait_ge(pv_done, l * UNITS + end)
                    if g >= 2:
                        dve.wait_ge(ot_done, l * 2 * TT + (g - 1))
                    link(l, V.reciprocal(rinv[:, end - n:end], rowsum[:, end - n:end]))
                    o = o_sb[:, is_mem * T:is_mem * T + n * HD].rearrange("p (h d) -> p h d", d=HD)
                    ps = bank[4 + is_mem][:, 0:n * HD].rearrange("p (h d) -> p h d", d=HD)
                    ri = rinv[:, end - n:end].rearrange("p (h d) -> p h d", d=1).broadcast_to([P, n, HD])
                    V.tensor_tensor(out=o, in0=ps, in1=ri, op=ALU.mult).then_inc(o_ready, 1)

                def split_y(g):
                    i, is_mem = divmod(g, 2)
                    n = 2 if is_mem else 4
                    lo, hi = (t[:, (6 if is_mem else 0) * T:(8 if is_mem else 4) * T]
                              .rearrange("p (c t) -> p c t", t=T)[:, :, i * P:(i + 1) * P]
                              for t in (y_lo, y_hi))
                    dve.wait_ge(yt_hi, l * 2 * TT + (g + 1))
                    V.tensor_tensor(out=lo, in0=bank[6 + is_mem][:, 0:n * P]
                                    .rearrange("p (c t) -> p c t", t=P),
                                    in1=hi.bitcast(f32), op=ALU.subtract).then_inc(yt_lo, 1)

                for n in range(UNITS + 4):
                    if n < UNITS:
                        mask_and_max(n)
                    if n - 2 in group_after:
                        finish(group_after[n - 2])
                    if n - 4 + 1 in group_after:
                        split_y(group_after[n - 4 + 1])
                update(l, 1, ACC_BASE[1] + ACC * (DC - 1), MIX_BASE["out"] + DC, 1.0)

            dve.wait_ge(setup_loaded, 48)
            dve.sem_inc(x_new, DC)
            dve.sem_inc(gu_free, 2)
            with dve.Fori(0, LAYERS) as l:
                ffn(l, 0)
                mix(l)
                ffn(l, 1)
            assert links[0] == DVE_CHAIN, links[0]


def _constants():
    import numpy as np

    c = np.zeros((P, CONSTS), np.float32)
    p = np.arange(P)
    c[:, C_ID:C_ID + P] = np.eye(P)
    c[:, C_ONES:C_ONES + P] = 1
    c[:, C_BLOCK:C_BLOCK + P] = p[:, None] // HD == p[None, :] // HD
    c[:, C_CAUSAL + T - P:C_CAUSAL + T] = np.where(p[None, :] <= p[:, None], 0, NEG)
    for j in range(NORMED):
        for half in range(2):
            row = 2 * j + half
            c[half * HD:(half + 1) * HD, C_SEL + j * NROW + row] = 1
            c[row, C_SPREAD + j * P + half * HD:C_SPREAD + j * P + (half + 1) * HD] = 1
    for i in range(2):
        for half in range(2):
            w = WINDOWS[2 * i + half]
            s = slice(half * HD, (half + 1) * HD)
            c[s, C_INV + 16 * i:C_INV + 16 * (i + 1)] = 1 / np.minimum(np.arange(16) + 1, w)
            c[s, C_INVW + i] = 1 / w
    c[:, C_EPS] = EPS
    return c


def _by_output(w, n):
    return w.reshape(DC, P, n, P).transpose(2, 1, 0, 3).reshape(n, P, SLOT)


def _weight_stream(a, l):
    import numpy as np

    def ffn(gate, up, down):
        gu = np.stack([_by_output(gate, FC), _by_output(up, FC)], 1).reshape(2 * FC, P, SLOT)
        return [gu, down.reshape(FC, P, SLOT)]

    def by_tokens(w, chunks):
        return w.reshape(DC // chunks, chunks, P, -1).transpose(0, 2, 1, 3).reshape(-1, P, SLOT)

    w = a["w_in"][l]
    at = np.cumsum([0, 512, 512, 512, 256, 64, 4, 256, 256])
    aq, ak, av, iq, ik, iw, pu, mq = (w[:, at[i]:at[i + 1]] for i in range(8))
    kv = a["w_mem_kv"][l]
    iw = np.concatenate([iw, np.zeros((D, P - 4), iw.dtype)], 1)
    parts = ffn(a["ffn1_gate"][l], a["ffn1_up"][l], a["ffn1_down"][l])
    parts += [_by_output(iq, 2), _by_output(np.concatenate([ik, ik], 1), 1), _by_output(iw, 1),
              by_tokens(av, 2), _by_output(aq, 4), _by_output(ak, 4), _by_output(mq, 2),
              _by_output(pu, 2), _by_output(kv[:, :256], 2), by_tokens(kv[:, 256:], 4),
              a["w_out"][l].reshape(DC, P, SLOT)]
    parts += ffn(a["ffn2_gate"][l], a["ffn2_up"][l], a["ffn2_down"][l])
    return parts


def kernel(**inputs):
    import numpy as np
    import concourse.bacc as bacc
    from concourse.bass_utils import run_bass_kernel_spmd

    a = {k: np.asarray(v) for k, v in inputs.items()}

    def transposed(m):
        return m.reshape(-1, DC, P).transpose(2, 1, 0).reshape(P, -1)

    params = []
    pool_w = np.zeros((LAYERS, P, 2 * P), np.float32)
    for l in range(LAYERS):
        for name in ("ffn1_norm", "mix_norm", "ffn2_norm", "mem_norm"):
            params.append(a[name][l].reshape(DC, P).T)
        for name in ("q_norm", "k_norm", "mq_norm", "mk_norm"):
            params.append(np.concatenate([a[name][l]] * 2)[:, None])
        params.append(a["pool_scale"][l].reshape(2, P).T)
        for g in range(4):
            i, half = divmod(g, 2)
            pool_w[l, half * HD:(half + 1) * HD, i * P + half * HD:i * P + (half + 1) * HD] = a["w_pool"][l, g]
    data = {
        "x_t": transposed(a["x"][0]),
        "mem_t": transposed(a["mem"][0]),
        "weights": np.concatenate([p for l in range(LAYERS) for p in _weight_stream(a, l)], 0),
        "pool_w": pool_w,
        "params": np.concatenate(params, 1),
        "consts": _constants(),
    }
    nc = bacc.Bacc("TRN2", target_bir_lowering=False, num_devices=1)
    arrays, args = {}, []
    for name, v in data.items():
        arrays[name] = np.ascontiguousarray(v)
        args.append(nc.dram_tensor(name, arrays[name].shape, mybir.dt.from_np(arrays[name].dtype),
                                   kind="ExternalInput").ap())
    out = nc.dram_tensor("out_t", (P, DC * T), mybir.dt.float32, kind="ExternalOutput").ap()
    build(nc, *args, out)
    res = run_bass_kernel_spmd(nc, [arrays], core_ids=[0])
    got = res.results[0]["out_t"].reshape(P, DC, T).transpose(2, 1, 0).reshape(1, T, D)
    return np.ascontiguousarray(got)
```

```python
import concourse.bass as bass
from concourse import mybir

P = 128
D = 1024
T = 512
LAYERS = 2
HD = 64
HEADS = 8
IDX_HEADS = 4
MEM_HEADS = 4
MEM = 256
FF = 2816
TOPK = min(256, T // 4)
WINDOWS = (2, 4, 8, 16)
EPS = 1e-6

DC = D // P
TT = T // P
MT = MEM // P
FC = FF // P
SLOT = DC * P
RING = 4

MIX_SLOTS = (("iq", 2), ("ik", 1), ("iw", 1), ("av", 4), ("aq", 4), ("ak", 4), ("mk", 2), ("mq", 2),
             ("pu", 2), ("mv", 2), ("out", 8))
FFN_SLOTS = 2 * FC + FC
MIX_BASE = {}
_at = FFN_SLOTS
for _name, _n in MIX_SLOTS:
    MIX_BASE[_name] = _at
    _at += _n
FFN_BASE = (0, _at)
SLOTS = _at + FFN_SLOTS
assert SLOTS % RING == 0

G_FFN1, G_MIX, G_FFN2, G_MEM = 0, DC, 2 * DC, 3 * DC
G_Q, G_K, G_MQ, G_MK, G_POOL = (4 * DC + i for i in range(5))
PARAMS = 4 * DC + 4 + 2

ZT = HEADS // 2 * 2 + MEM_HEADS // 2
NORMED = ZT + MEM_HEADS // 2
NROW = 2 * NORMED
C_ID = 0
C_ONES = C_ID + P
C_BLOCK = C_ONES + P
C_CAUSAL = C_BLOCK + P
C_SEL = C_CAUSAL + T
C_SPREAD = C_SEL + NORMED * NROW
C_INV = C_SPREAD + NORMED * P
C_INVW = C_INV + 2 * 16
C_EPS = C_INVW + 2
CONSTS = C_EPS + 1

X_PARTS = 4
NEG = -1e30
TAKEN = -3e38
ROUNDS = TOPK // 8
ROUNDS_PER_STEP = 4
PAD = 16
UNITS_PER_TILE = HEADS + MEM_HEADS
UNITS = TT * UNITS_PER_TILE
POOL_UNIT = 6
ORDER = [0, 1, 2, 3, 4, 5, 6, 7, "mk", 8, 9]

POOL_CHAIN = 15
DVE_CHAIN = 112


def build(nc, x_t, mem_t, weights, pool_w, params, consts, out):
    f32, f32r = mybir.dt.float32, mybir.dt.float32r
    ALU, ACT = mybir.AluOpType, mybir.ActivationFunctionType
    ds = bass.ds

    base = -(-nc.sbuf_base // 64) * 64
    tile_b = T * 4

    def place(name, cols, at, dt=f32, parts=P):
        return nc.alloc_sbuf_tensor_at(name, [parts, cols], dt, offset=at)

    cursor = [base]

    def new(name, cols, dt=f32, parts=P):
        at = cursor[0]
        cursor[0] += -(-cols * 4 // 64) * 64
        return place(name, cols, at, dt, parts)

    x = new("x", DC * T)
    h_at = cursor[0]
    h_hi = new("h_hi", DC * T, f32r)
    h_lo = new("h_lo", DC * T, f32r)
    raw = new("raw", RING * SLOT)
    w_hi = new("w_hi", RING * SLOT, f32r)
    w_lo = new("w_lo", RING * SLOT, f32r)
    a_hi_at = cursor[0]
    a_hi = new("a_hi", FC * T, f32r)
    a_lo_at = cursor[0]
    a_lo = new("a_lo", FC * T, f32r)
    r = new("r", T)
    t1 = new("t1", 2 * T)
    t2 = new("t2", 2 * T)
    const = new("const", CONSTS)
    par = new("par", LAYERS * PARAMS)
    wpool = new("wpool", 2 * P)
    cols = new("cols", TT + TT * IDX_HEADS)
    rmem_col = new("rmem_col", MT)
    top8 = new("top8", 8)
    assert cursor[0] <= nc.sbuf_usable_end, cursor[0]
    y_hi, y_lo = a_hi, a_lo
    m_hi = a_hi[:, 8 * T:8 * T + DC * MEM]
    m_lo = a_lo[:, 8 * T:8 * T + DC * MEM]
    z = place("z", ZT * T, a_hi_at + 12 * tile_b)
    mem = place("mem", DC * MEM, a_hi_at)
    u = place("u", 2 * (PAD + T), a_hi_at + 4 * tile_b)
    wa = place("wa", PAD + T, a_hi_at + 4 * tile_b + 2 * (PAD + T) * 4)
    iq = place("iq", 2 * T, a_lo_at)
    ik = place("ik", T, a_lo_at + 2 * tile_b)
    iw = place("iw", T, a_lo_at + 3 * tile_b)
    wb = place("wb", PAD + T, a_lo_at + 4 * tile_b)
    hrms = place("hrms", T, a_lo_at + 6 * tile_b, parts=NROW)
    v = place("v", TT * T, a_lo_at + 12 * tile_b)
    mk = place("mk", 2 * MEM, a_lo_at + 16 * tile_b)
    mv = place("mv", MT * MEM, a_lo_at + 17 * tile_b)
    score_at = [0, 0, 2 * P, 5 * P]
    score = place("score", 9 * P, a_lo_at + 18 * tile_b)
    small = a_lo_at + 21 * tile_b
    rmem = place("rmem", MEM, small)
    rowmax, negmax, rowsum, rinv = (
        place(name, UNITS, small + (MEM + i * UNITS) * 4)
        for i, name in enumerate(("rowmax", "negmax", "rowsum", "rinv")))
    sq = place("sq", DC * T, a_lo_at + 14 * tile_b)
    pt = place("pt", 2 * T, h_at)
    o_sb = place("o_sb", 2 * T, h_at + 2 * tile_b)

    bank = [nc.alloc_psum_tensor(f"bank{i}", [P, 512], f32) for i in range(8)]

    def chunk(t, j, n=T, size=None):
        return t[:, j * n:j * n + (size or n)]

    def con(at, n=1, parts=P):
        return const[0:parts, at:at + n]

    def sem(name):
        return nc.alloc_semaphore(name)

    w_loaded = [sem(f"w_loaded{i}") for i in range(RING)]
    w_hi_done = sem("w_hi_done")
    w_ready = sem("w_ready")
    slot_done = sem("slot_done")
    acc_done = sem("acc_done")
    params_loaded = sem("params_loaded")
    consts_loaded = sem("consts_loaded")
    x_loaded = [sem(f"x_loaded{q}") for q in range(X_PARTS)]
    mem_loaded = sem("mem_loaded")
    pool_w_loaded = sem("pool_w_loaded")
    out_stored = sem("out_stored")
    x_new = sem("x_new")
    hi_ready = sem("hi_ready")
    lo_ready = sem("lo_ready")
    sq_ready = sem("sq_ready")
    ssq_ready = sem("ssq_ready")
    sum_done = sem("sum_done")
    rms_ready = sem("rms_ready")
    r_ready = sem("r_ready")
    gate_ready = sem("gate_ready")
    gu_free = sem("gu_free")
    silu_ready = sem("silu_ready")
    prod_ready = sem("prod_ready")
    a_hi_ready = sem("a_hi_ready")
    a_lo_ready = sem("a_lo_ready")
    proj_ready = sem("proj_ready")
    msq_ready = sem("msq_ready")
    mssq_ready = sem("mssq_ready")
    msum_done = sem("msum_done")
    mrms_ready = sem("mrms_ready")
    rmem_ready = sem("rmem_ready")
    m_hi_ready = sem("m_hi_ready")
    m_lo_ready = sem("m_lo_ready")
    cols_done = sem("cols_done")
    cols_ready = sem("cols_ready")
    mcols_done = sem("mcols_done")
    mcols_ready = sem("mcols_ready")
    v_ready = sem("v_ready")
    mv_ready = sem("mv_ready")
    dots_done = sem("dots_done")
    relu_ready = sem("relu_ready")
    acc_score = sem("acc_score")
    bias_ready = sem("bias_ready")
    zsq_ready = sem("zsq_ready")
    zsum_done = sem("zsum_done")
    hrms_ready = sem("hrms_ready")
    hinv_ready = sem("hinv_ready")
    spread_done = sem("spread_done")
    zn_ready = sem("zn_ready")
    pooled_ready = sem("pooled_ready")
    pool_done = sem("pool_done")
    ypool_hi = sem("ypool_hi")
    ypool_lo = sem("ypool_lo")
    logit_done = sem("logit_done")
    lm_ready = sem("lm_ready")
    nm_ready = sem("nm_ready")
    p_ready = sem("p_ready")
    ptp_done = sem("ptp_done")
    pt_ready = sem("pt_ready")
    pv_done = sem("pv_done")
    o_ready = sem("o_ready")
    ot_done = sem("ot_done")
    yt_hi = sem("yt_hi")
    yt_lo = sem("yt_lo")
    dve_chain = sem("dve_chain")
    pool_chain = sem("pool_chain")

    ACC = 7
    ACC_BASE = (0, FC * ACC, FC * ACC + 8 * ACC)
    ACC_LAYER = ACC * (2 * FC + 8)

    def unit(n):
        i, h = divmod(n, UNITS_PER_TILE)
        is_mem = h >= HEADS
        return i, (h - HEADS if is_mem else h), is_mem, (MT if is_mem else i + 1)

    def group_end(g):
        i, is_mem = divmod(g, 2)
        return i * UNITS_PER_TILE + (UNITS_PER_TILE if is_mem else HEADS)

    group_after = {group_end(g): g for g in range(2 * TT)}

    passed = sem("passed")

    def wait_apart(eng, s, value):
        eng.wait_ge(s, value)
        eng.sem_inc(passed, 1)

    with nc.Block() as block:

        @block.sync
        def _(sp):
            def load(n, pos, first=False):
                if not first:
                    sp.wait_ge(w_ready, n + (1 - RING))
                src = weights[ds(n, 1), :, :].rearrange("a p n -> (a p) n")
                sp.dma_start(raw[:, pos * SLOT:(pos + 1) * SLOT], src).then_inc(w_loaded[pos], 16)

            load(0, 0, first=True)
            load(1, 1, first=True)
            sp.dma_start(const[:, :], consts[:, :]).then_inc(consts_loaded, 16)
            load(2, 2, first=True)
            load(3, 3, first=True)
            with sp.Fori(1, LAYERS * SLOTS // RING + 1) as i:
                for pos in range(RING):
                    load(i * RING + pos, pos)
            for pos in range(RING):
                sp.wait_ge(w_loaded[pos], 16 * (LAYERS * SLOTS // RING + 1))
            for j in range(DC):
                sp.wait_ge(x_new, 3 * DC * LAYERS + j + 1)
                sp.dma_start(out[:, j * T:(j + 1) * T], chunk(x, j)).then_inc(out_stored, 16)
            sp.wait_ge(out_stored, 16 * DC)

        @block.gpsimd
        def _(pool):
            G = nc.gpsimd
            steps = [0]

            def rest(l, n):
                pos = n[1] % RING
                s = slice(pos * SLOT, (pos + 1) * SLOT)
                pool.wait_ge(w_hi_done, l * SLOTS + n[0] + (n[1] + 1))
                G.tensor_tensor(out=w_lo[:, s], in0=raw[:, s], in1=w_hi[:, s].bitcast(f32),
                                op=ALU.subtract).then_inc(w_ready, 1)

            def step(l, ins):
                steps[0] += 1
                ins.then_inc(pool_chain, 1)
                pool.wait_ge(pool_chain, l * POOL_CHAIN + steps[0])

            def pooling(l):
                wait_apart(pool, proj_ready, (l + 1) * 17)
                for t in (u[:, 0:PAD], u[:, PAD + T:2 * PAD + T], wa[:, 0:PAD]):
                    G.memset(t, 0.0)
                step(l, G.memset(wb[:, 0:PAD], 0.0))
                for i in range(2):
                    ui = u[:, i * (PAD + T):(i + 1) * (PAD + T)]

                    def shifted_sum(p0, dst, src, by):
                        step(l, G.tensor_tensor(out=dst[p0:P, PAD:PAD + T], in0=src[p0:P, PAD:PAD + T],
                                                in1=src[p0:P, PAD - by:PAD + T - by], op=ALU.add))

                    shifted_sum(0, wa, ui, 1)
                    if i == 0:
                        shifted_sum(HD, wb, wa, 2)
                    else:
                        shifted_sum(0, wb, wa, 2)
                        shifted_sum(0, wa, wb, 4)
                        shifted_sum(HD, wb, wa, 8)
                    for half, w in enumerate((wa, wb)):
                        p = slice(half * HD, (half + 1) * HD)
                        G.tensor_tensor(out=w[p, PAD:PAD + 16], in0=w[p, PAD:PAD + 16],
                                        in1=const[p, C_INV + 16 * i:C_INV + 16 * (i + 1)], op=ALU.mult)
                        step(l, G.tensor_scalar(w[p, PAD + 16:PAD + T], w[p, PAD + 16:PAD + T],
                                                const[p, C_INVW + i:C_INVW + i + 1], None, ALU.mult))
                        step(l, G.tensor_tensor(out=ui[p, PAD:PAD + T], in0=w[p, PAD:PAD + T],
                                                in1=ui[p, PAD:PAD + T], op=ALU.subtract))
                    pool.sem_inc(pooled_ready, 1)

            ahead = MIX_BASE["out"] + RING
            with pool.Fori(0, LAYERS) as l:
                with pool.Fori(0, ahead // RING) as i:
                    for pos in range(RING):
                        rest(l, (i * RING, pos))
                for n in range(ahead // RING * RING, ahead):
                    rest(l, (0, n))
                pool.wait_ge(consts_loaded, 16)
                pooling(l)
                first = -(-ahead // RING) * RING
                for n in range(ahead, first):
                    rest(l, (0, n))
                with pool.Fori(0, (SLOTS - first) // RING) as i:
                    for pos in range(RING):
                        rest(l, (i * RING, first + pos))
            assert steps[0] == POOL_CHAIN, steps[0]

        @block.tensor
        def _(pe):
            def mm(out_, lhsT, rhs, start=True, stop=True):
                return nc.tensor.matmul(out_, lhsT, rhs, start=start, stop=stop, skip_group_check=True)

            def passes(out_, w, act, start, stop):
                (whi, wlo), (ahi, alo) = w, act
                mm(out_, whi, ahi, start, False)
                mm(out_, whi, alo, False, False)
                return mm(out_, wlo, ahi, False, stop)

            def weight(pos, at, n=P):
                s = slice(pos * SLOT + at, pos * SLOT + at + n)
                return w_hi[:, s], w_lo[:, s]

            def pair(hi, lo, at, n=T):
                return hi[:, at:at + n], lo[:, at:at + n]

            def project(l, n, to, hi, lo, width=T, lo_sem=None):
                pe.wait_ge(w_ready, l * SLOTS + (n + 1))
                for k in range(DC):
                    if lo_sem is not None:
                        pe.wait_ge(lo_ready, lo_sem + (k + 1))
                    last = passes(to, weight(n % RING, k * P), pair(hi, lo, k * width, width),
                                  k == 0, k == DC - 1)
                last.then_inc(slot_done, 1)

            def token_sums(l, ph):
                pe.wait_ge(ssq_ready, l * 3 + (ph + 1))
                mm(bank[4][:, :], con(C_ONES, P), chunk(sq, 0)).then_inc(sum_done, 1)

            def accumulate(pos, hi, lo, start, stop):
                for j in range(DC):
                    last = passes(bank[j][:, :], weight(pos, j * P), (hi, lo), start, stop)
                    if j < ACC:
                        last.then_inc(acc_done, 1)
                    else:
                        last.then_inc(slot_done, 1)

            def ffn(l, e):
                ph, ffn_at = 2 * e, FFN_BASE[e]
                def gate_up(f, half, first=False):
                    n = ffn_at + 2 * half
                    pe.wait_ge(gu_free, (l * 2 + e) * FC + (f + (half + 1)))
                    at = l * SLOTS + ffn_at + f * 2 + 2 * half
                    for up in range(2):
                        pos = (n + up) % RING
                        pe.wait_ge(w_ready, at + (up + 1))
                        for k in range(DC):
                            if first and half == 0 and up == 0:
                                pe.wait_ge(lo_ready, (l * 3 + ph) * DC + (k + 1))
                            last = passes(bank[2 * half + up][:, :], weight(pos, k * P),
                                          pair(h_hi, h_lo, k * T), k == 0, k == DC - 1)
                        last.then_inc(slot_done, 1)
                    if first and half == 0:
                        token_sums(l, ph)

                gate_up(0, 0, first=True)
                gate_up(0, 1)
                with pe.Fori(1, FC // 2) as i:
                    gate_up(i * 2, 0)
                    gate_up(i * 2, 1)

                down_at = ffn_at + 2 * FC
                def down(f, off, start=False, stop=False):
                    at = l * SLOTS + down_at + f + off
                    pe.wait_ge(w_ready, at + 1)
                    pe.wait_ge(a_lo_ready, (l * 2 + e) * FC + (f + (off + 1)))
                    fo = f * T + off * T
                    pos = (down_at + off + (f if isinstance(f, int) else 0)) % RING
                    accumulate(pos, a_hi[:, ds(fo, T)], a_lo[:, ds(fo, T)], start, stop)

                pe.wait_ge(rms_ready, l * 3 + (ph + 1))
                pe.wait_ge(gu_free, (l * 2 + e) * FC + (FC + 2))
                down(0, 0, start=True)
                down(0, 1)
                with pe.Fori(0, (FC - 2) // RING - 1) as i:
                    for off in range(RING):
                        down(i * RING, 2 + off)
                for off in range(RING):
                    down(FC - RING, off, stop=off == RING - 1)

            def mix(l):
                def at(name, i=0):
                    return MIX_BASE[name] + i

                def heads_sum(j):
                    pe.wait_ge(zsq_ready, l * (ZT + 1) + (j + 1))
                    if ORDER[j] == "mk":
                        for i in range(2):
                            last = mm(bank[6][0:NROW, 0:MEM], con(C_SEL + (ZT + i) * NROW, NROW),
                                      t1[:, (j % 2) * T + i * MEM:(j % 2) * T + (i + 1) * MEM],
                                      False, False)
                    else:
                        last = mm(bank[6][0:NROW, :], con(C_SEL + ORDER[j] * NROW, NROW),
                                  chunk(t1, j % 2), j == 0, j == ZT)
                    last.then_inc(zsum_done, 1)

                project(l, at("iq", 0), bank[0][:, :], h_hi, h_lo, lo_sem=(l * 3 + 1) * DC)
                project(l, at("iq", 1), bank[1][:, :], h_hi, h_lo)
                token_sums(l, 1)
                project(l, at("ik"), bank[2][:, :], h_hi, h_lo)
                project(l, at("iw"), bank[3][:, :], h_hi, h_lo)
                pe.wait_ge(rms_ready, l * 3 + 2)

                def project_v(s):
                    n = at("av", s)
                    pe.wait_ge(w_ready, l * SLOTS + (n + 1))
                    for half in range(2):
                        k = 2 * s + half
                        whi, wlo = weight(n % RING, half * T, T)
                        for i in range(TT):
                            hhi, hlo = pair(h_hi, h_lo, k * T + i * P, P)
                            last = passes(bank[4 + i][:, :], (hhi, hlo), (whi, wlo),
                                          k == 0, k == DC - 1)
                    last.then_inc(slot_done, 1)

                project_v(0)
                project_v(1)
                pe.wait_ge(proj_ready, l * 17 + 4)
                for i in range(TT):
                    mm(bank[3][:, i:i + 1], r[0:1, i * P:(i + 1) * P], con(C_ONES, 1, 1))
                for i in range(TT):
                    last = mm(bank[3][:, TT + 4 * i:TT + 4 * i + 4], iw[0:4, i * P:(i + 1) * P],
                              con(C_ID, 4, 4))
                last.then_inc(cols_done, 1)
                n = 0
                for i in range(1, TT):
                    for h in range(IDX_HEADS):
                        if n >= 2:
                            pe.wait_ge(relu_ready, l * 12 + (n - 1))
                        p0 = HD * (h % 2)
                        mm(bank[n % 2][:, 0:(i + 1) * P],
                           iq[p0:p0 + HD, (h // 2) * T + i * P:(h // 2) * T + (i + 1) * P],
                           ik[p0:p0 + HD, 0:(i + 1) * P]).then_inc(dots_done, 1)
                        n += 1
                project_v(2)
                project_v(3)
                pe.wait_ge(mssq_ready, l + 1)
                mm(bank[2][:, 0:MEM], con(C_ONES, P), sq[:, 0:MEM]).then_inc(msum_done, 1)

                def project_z(t, name, i):
                    if t < 6:
                        pe.wait_ge(relu_ready, (l + 1) * 12)
                    elif t == 6:
                        pe.wait_ge(mrms_ready, l + 1)
                    elif t == 7:
                        pe.wait_ge(cols_ready, l + 1)
                    else:
                        pe.wait_ge(proj_ready, l * 17 + (t - 3 + (t - 4 >= 12)))
                    project(l, at(name, i), bank[t % 4][:, :], h_hi, h_lo)

                for i in range(4):
                    project_z(4 + i, "aq", i)
                    if i >= 2:
                        heads_sum(i - 2)
                for i in range(4):
                    project_z(8 + i, "ak", i)
                    heads_sum(2 + i)
                pe.wait_ge(m_lo_ready, l + 1)
                pe.wait_ge(v_ready, (l + 1) * TT)
                for i in range(2):
                    project(l, at("mk", i), bank[4][:, i * MEM:(i + 1) * MEM], m_hi, m_lo, MEM)
                heads_sum(6)
                pe.wait_ge(rmem_ready, l + 1)
                for i in range(MT):
                    last = mm(bank[7][:, i:i + 1], rmem[0:1, i * P:(i + 1) * P], con(C_ONES, 1, 1))
                last.then_inc(mcols_done, 1)
                project_z(12, "mq", 0)
                heads_sum(7)
                project_z(13, "mq", 1)
                heads_sum(8)
                project_z(14, "pu", 0)
                heads_sum(9)
                project_z(15, "pu", 1)
                heads_sum(10)
                pe.wait_ge(w_ready, l * SLOTS + (at("mv") + 2))
                for i in range(MT):
                    for k in range(DC):
                        s, q = divmod(k, 4)
                        last = passes(bank[5][:, i * MEM:(i + 1) * MEM],
                                      pair(m_hi, m_lo, k * MEM + i * P, P),
                                      weight(at("mv", s) % RING, q * MEM, MEM), k == 0, k == DC - 1)
                        if i == MT - 1 and q == 3:
                            last.then_inc(slot_done, 1)
                pe.wait_ge(hinv_ready, l + 1)
                for j in range(NORMED):
                    if j < 3:
                        pe.wait_ge(proj_ready, l * 17 + (14 + j))
                    else:
                        pe.wait_ge(zn_ready, l * NORMED + (j - 2))
                    n = T if j < ZT else MEM
                    mm(bank[j % 3][:, 0:n], con(C_SPREAD + j * P, P, NROW), hrms[:, 0:n])\
                        .then_inc(spread_done, 1)

                def pool_maps():
                    pe.wait_ge(pool_w_loaded, (l + 1) * 16)
                    pe.wait_ge(pooled_ready, (l + 1) * 2)
                    pe.wait_ge(mcols_ready, l + 1)
                    for i in range(2):
                        mm(bank[6 + i][:, :], chunk(wpool, i, P),
                           u[:, i * (PAD + T) + PAD:(i + 1) * (PAD + T)]).then_inc(pool_done, 1)

                pe.wait_ge(zn_ready, (l + 1) * NORMED)
                pe.wait_ge(mv_ready, (l + 1) * MT)
                pe.wait_ge(proj_ready, (l + 1) * 17)

                def logits(n):
                    i, h, is_mem, blocks = unit(n)
                    if n >= 2:
                        pe.wait_ge(lm_ready, l * UNITS + (n - 1))
                    p0, j = HD * (h % 2), h // 2
                    if is_mem:
                        qt, kt = HEADS + j, mk[p0:p0 + HD, j * MEM:(j + 1) * MEM]
                    else:
                        qt, kt = j, z[p0:p0 + HD, (4 + j) * T:(4 + j) * T + blocks * P]
                    mm(bank[n % 2][:, 0:blocks * P],
                       z[p0:p0 + HD, qt * T + i * P:qt * T + (i + 1) * P], kt).then_inc(logit_done, 1)

                def transpose_p(n):
                    i, h, is_mem, blocks = unit(n)
                    pe.wait_ge(p_ready, l * UNITS + (n + 1))
                    if n >= 2:
                        pe.wait_ge(pt_ready, l * UNITS + (n - 1))
                    for b in range(blocks):
                        last = nc.tensor.transpose(bank[2 + n % 2][:, b * P:(b + 1) * P],
                                                   t1[:, (n % 2) * T + b * P:(n % 2) * T + (b + 1) * P],
                                                   con(C_ID, P))
                    last.then_inc(ptp_done, 1)

                def times_v(n):
                    i, h, is_mem, blocks = unit(n)
                    pe.wait_ge(pt_ready, l * UNITS + (n + 1))
                    if h == 0 and i > 0:
                        pe.wait_ge(o_ready, l * 2 * TT + (2 * i - 1 + is_mem))
                    for b in range(blocks):
                        val = mv[:, b * MEM + h * HD:b * MEM + (h + 1) * HD] if is_mem else \
                            v[:, b * T + h * HD:b * T + (h + 1) * HD]
                        last = mm(bank[4 + is_mem][:, h * HD:(h + 1) * HD],
                                  pt[:, (n % 2) * T + b * P:(n % 2) * T + (b + 1) * P], val,
                                  b == 0, b == blocks - 1)
                    last.then_inc(pv_done, 1)

                def transpose_o(g):
                    i, is_mem = divmod(g, 2)
                    pe.wait_ge(o_ready, l * 2 * TT + (g + 1))
                    if g >= 2:
                        pe.wait_ge(yt_lo, l * 2 * TT + (g - 1))
                    else:
                        pe.wait_ge(ypool_lo, (l + 1) * 2)
                    for b in range(2 if is_mem else 4):
                        last = nc.tensor.transpose(bank[6 + is_mem][:, b * P:(b + 1) * P],
                                                   o_sb[:, is_mem * T + b * P:is_mem * T + (b + 1) * P],
                                                   con(C_ID, P))
                    last.then_inc(ot_done, 1)

                for n in range(UNITS + 3):
                    if n == POOL_UNIT:
                        pool_maps()
                    if n < UNITS:
                        logits(n)
                    if 0 <= n - 1 < UNITS:
                        transpose_p(n - 1)
                    if 0 <= n - 2 < UNITS:
                        times_v(n - 2)
                    if n - 3 + 1 in group_after:
                        transpose_o(group_after[n - 3 + 1])

                pe.wait_ge(yt_lo, (l + 1) * 2 * TT)
                for k in range(DC):
                    n = at("out", k)
                    pe.wait_ge(w_ready, l * SLOTS + (n + 1))
                    accumulate(n % RING, chunk(y_hi, k), chunk(y_lo, k), k == 0, k == DC - 1)

            pe.sem_inc(slot_done, RING)
            pe.wait_ge(consts_loaded, 16)
            with pe.Fori(0, LAYERS) as l:
                ffn(l, 0)
                mix(l)
                ffn(l, 1)

        @block.scalar
        def _(act):
            def prepare(l, ph, gain, last_slot):
                for j in range(DC):
                    act.wait_ge(x_new, (l * 3 + ph) * DC + (j + 1))
                    nc.scalar.activation(chunk(h_hi, j), chunk(x, j), ACT.Copy,
                                         scale=par[:, ds(l * PARAMS + (gain + j), 1)])\
                        .then_inc(hi_ready, 1)
                round_ahead(l, last_slot)
                for half in range(2):
                    s = slice(half * 4 * T, (half + 1) * 4 * T)
                    nc.scalar.activation(sq[:, s], x[:, s], ACT.Square).then_inc(sq_ready, 1)

            def root(l, ph):
                act.wait_ge(sum_done, l * 3 + (ph + 1))
                nc.scalar.activation(r[:, :], bank[4][:, :], ACT.Sqrt, bias=con(C_EPS),
                                     scale=1.0 / D).then_inc(rms_ready, 1)

            def round_ahead(l, n, off=0):
                pos = (n + RING) % RING
                s = slice(pos * SLOT, (pos + 1) * SLOT)
                act.wait_ge(slot_done, l * SLOTS + off + (n + RING + 1))
                act.wait_ge(w_loaded[pos], 16 * (SLOTS // RING) * l + off * (16 // RING)
                            + 16 * ((n + RING) // RING + 1))
                nc.scalar.activation(w_hi[:, s], raw[:, s], ACT.Copy).then_inc(w_hi_done, 1)

            def ffn(l, e):
                at = FFN_BASE[e]
                prepare(l, 2 * e, (G_FFN1, G_FFN2)[e], at - 1)
                root(l, 2 * e)
                with act.Fori(0, FC // 2) as i:
                    f = i * 2
                    for half in range(2):
                        done = (l * 2 + e) * FC + f + (half + 1)
                        g = chunk(t1, half)
                        round_ahead(l, at + 2 * half, f * 2)
                        act.wait_ge(gate_ready, done)
                        nc.scalar.activation(g, g, ACT.Silu).then_inc(silu_ready, 1)
                        round_ahead(l, at + 2 * half + 1, f * 2)
                        act.wait_ge(prod_ready, done)
                        nc.scalar.activation(a_hi[:, ds(f * T + half * T, T)], chunk(t2, half),
                                             ACT.Copy).then_inc(a_hi_ready, 1)
                down = at + 2 * FC
                with act.Fori(0, (FC - 1) // RING) as i:
                    for off in range(RING):
                        round_ahead(l, down + off, i * RING)
                for n in range((FC - 1) // RING * RING, FC - 1):
                    round_ahead(l, down + n)

            def mix(l):
                prepare(l, 1, G_MIX, MIX_BASE["iq"] - 1)
                round_ahead(l, MIX_BASE["iq"])
                act.dma_start(mem[:, :], mem_t[:, :]).then_inc(mem_loaded, 16)
                act.dma_start(wpool[:, :], pool_w[ds(l, 1), :, :].rearrange("a p n -> (a p) n"))\
                    .then_inc(pool_w_loaded, 16)
                round_ahead(l, MIX_BASE["iq"] + 1)
                root(l, 1)
                act.wait_ge(mem_loaded, (l + 1) * 16)
                for j in range(DC):
                    s = slice(j * MEM, (j + 1) * MEM)
                    nc.scalar.activation(m_hi[:, s], mem[:, s], ACT.Copy,
                                         scale=par[:, ds(l * PARAMS + (G_MEM + j), 1)])\
                        .then_inc(m_hi_ready, 1)
                round_ahead(l, MIX_BASE["ik"])
                nc.scalar.activation(sq[:, 0:DC * MEM], mem[:, :], ACT.Square).then_inc(msq_ready, 1)
                round_ahead(l, MIX_BASE["iw"])
                round_ahead(l, MIX_BASE["av"])
                round_ahead(l, MIX_BASE["av"] + 1)
                n = 0
                for i in range(1, TT):
                    for h in range(IDX_HEADS):
                        act.wait_ge(dots_done, l * 12 + (n + 1))
                        if n >= 2:
                            act.wait_ge(acc_score, l * 12 + (n - 1))
                        nc.scalar.activation(chunk(t2, n % 2, T, (i + 1) * P), bank[n % 2][:, 0:(i + 1) * P],
                                             ACT.Relu, scale=HD ** -0.5 * IDX_HEADS ** -0.5)\
                            .then_inc(relu_ready, 1)
                        n += 1
                round_ahead(l, MIX_BASE["av"] + 2)
                round_ahead(l, MIX_BASE["av"] + 3)
                act.wait_ge(msum_done, l + 1)
                nc.scalar.activation(rmem[:, :], bank[2][:, 0:MEM], ACT.Sqrt, bias=con(C_EPS),
                                     scale=1.0 / D).then_inc(mrms_ready, 1)
                act.wait_ge(cols_ready, l + 1)
                for i in range(TT):
                    nc.scalar.activation(chunk(v, i), bank[4 + i][:, :], ACT.Copy,
                                         scale=cols[:, i:i + 1]).then_inc(v_ready, 1)

                def squares(j):
                    act.wait_ge(proj_ready, l * 17 + (5 + j))
                    if j >= 2:
                        act.wait_ge(zsum_done, l * (ZT + 1) + (j - 1))
                    src = mk[:, :] if ORDER[j] == "mk" else chunk(z, ORDER[j])
                    nc.scalar.activation(chunk(t1, j % 2), src, ACT.Square).then_inc(zsq_ready, 1)

                slot = MIX_BASE["aq"]
                for j in range(ZT + 1):
                    for _ in range(2 if ORDER[j] == "mk" else 1):
                        round_ahead(l, slot)
                        slot += 1
                    squares(j)
                round_ahead(l, slot)
                act.wait_ge(zsum_done, (l + 1) * (ZT + 1))
                nc.scalar.activation(hrms[:, :], bank[6][0:NROW, :], ACT.Sqrt, bias=con(C_EPS, 1, NROW),
                                     scale=1.0 / HD).then_inc(hrms_ready, 1)
                for n in range(slot + 1, MIX_BASE["out"]):
                    round_ahead(l, n)
                act.wait_ge(mcols_ready, l + 1)
                for i in range(MT):
                    nc.scalar.activation(chunk(mv, i, MEM), chunk(bank[5], i, MEM), ACT.Copy,
                                         scale=rmem_col[:, i:i + 1]).then_inc(mv_ready, 1)
                def pool_hi():
                    act.wait_ge(pool_done, (l + 1) * 2)
                    for i in range(2):
                        nc.scalar.activation(chunk(y_hi, 4 + i), bank[6 + i][:, :], ACT.Copy,
                                             scale=par[:, ds(l * PARAMS + (G_POOL + i), 1)])\
                            .then_inc(ypool_hi, 1)

                def exps(n):
                    i, h, is_mem, blocks = unit(n)
                    act.wait_ge(nm_ready, l * UNITS + (n + 1))
                    if n >= 2:
                        act.wait_ge(ptp_done, l * UNITS + (n - 1))
                    nc.scalar.activation(chunk(t1, n % 2, T, blocks * P), chunk(t2, n % 2, T, blocks * P),
                                         ACT.Exp, bias=negmax[:, n:n + 1], scale=HD ** -0.5,
                                         accum_out=rowsum[:, n:n + 1]).then_inc(p_ready, 1)

                def copy_pt(n):
                    blocks = unit(n)[3]
                    act.wait_ge(ptp_done, l * UNITS + (n + 1))
                    if n >= 2:
                        act.wait_ge(pv_done, l * UNITS + (n - 1))
                    nc.scalar.activation(chunk(pt, n % 2, T, blocks * P), bank[2 + n % 2][:, 0:blocks * P],
                                         ACT.Copy).then_inc(pt_ready, 1)

                def split_y(g):
                    i, is_mem = divmod(g, 2)
                    n = 2 if is_mem else 4
                    y = y_hi[:, (6 if is_mem else 0) * T:(8 if is_mem else 4) * T]
                    act.wait_ge(ot_done, l * 2 * TT + (g + 1))
                    nc.scalar.activation(y.rearrange("p (c t) -> p c t", t=T)[:, :, i * P:(i + 1) * P],
                                         bank[6 + is_mem][:, 0:n * P].rearrange("p (c t) -> p c t", t=P),
                                         ACT.Copy).then_inc(yt_hi, 1)

                for n in range(UNITS + 4):
                    if n < UNITS:
                        exps(n)
                    if n == POOL_UNIT + 1:
                        pool_hi()
                    if 0 <= n - 1 < UNITS:
                        copy_pt(n - 1)
                    if n - 4 + 1 in group_after:
                        split_y(group_after[n - 4 + 1])
                for k in range(DC - 1):
                    round_ahead(l, MIX_BASE["out"] + k)

            act.dma_start(par[:, :], params[:, :]).then_inc(params_loaded, 16)
            for q in range(X_PARTS):
                s = slice(q * DC // X_PARTS * T, (q + 1) * DC // X_PARTS * T)
                act.dma_start(x[:, s], x_t[:, s]).then_inc(x_loaded[q], 16)
            for pos in range(RING - 1):
                round_ahead(0, pos - RING)
            act.wait_ge(params_loaded, 16)
            act.wait_ge(consts_loaded, 16)
            with act.Fori(0, LAYERS) as l:
                ffn(l, 0)
                mix(l)
                ffn(l, 1)

        @block.vector
        def _(dve):
            V = nc.vector
            links = [0]

            def link(l, ins):
                links[0] += 1
                ins.then_inc(dve_chain, 1)
                dve.wait_ge(dve_chain, l * DVE_CHAIN + links[0])

            def prepare(l, ph, gain):
                for j in range(DC):
                    dve.wait_ge(hi_ready, (l * 3 + ph) * DC + (j + 1))
                    V.scalar_tensor_tensor(out=chunk(h_lo, j), in0=chunk(x, j),
                                           scalar=par[:, ds(l * PARAMS + (gain + j), 1)],
                                           in1=chunk(h_hi, j).bitcast(f32), op0=ALU.mult,
                                           op1=ALU.subtract).then_inc(lo_ready, 1)
                dve.wait_ge(sq_ready, (l * 3 + ph) * 2 + 2)
                for half in (4 * T, 2 * T):
                    link(l, V.tensor_tensor(out=sq[:, 0:half], in0=sq[:, 0:half],
                                            in1=sq[:, half:2 * half], op=ALU.add))
                V.tensor_tensor(out=sq[:, 0:T], in0=sq[:, 0:T], in1=sq[:, T:2 * T],
                                op=ALU.add).then_inc(ssq_ready, 1)

            def invert(l, ph):
                dve.wait_ge(rms_ready, l * 3 + (ph + 1))
                V.reciprocal(r[:, :], r[:, :]).then_inc(r_ready, 1)
                wait_apart(dve, r_ready, l * 3 + (ph + 1))

            def update(l, ph, acc_at, slot_at, scale):
                for j in range(DC):
                    if j < ACC:
                        dve.wait_ge(acc_done, l * ACC_LAYER + (acc_at + j + 1))
                    else:
                        dve.wait_ge(slot_done, l * SLOTS + (RING + slot_at))
                    V.scalar_tensor_tensor(out=chunk(x, j), in0=bank[j][:, :], scalar=scale,
                                           in1=chunk(x, j), op0=ALU.mult, op1=ALU.add)\
                        .then_inc(x_new, 1)

            def ffn(l, e):
                ph = 2 * e
                prepare(l, ph, (G_FFN1, G_FFN2)[e])
                invert(l, ph)
                with dve.Fori(0, FC // 2) as i:
                    f = i * 2
                    for half in range(2):
                        done = (l * 2 + e) * FC + f + (half + 1)
                        slot = l * SLOTS + f * 2 + (RING + FFN_BASE[e] + 2 * half)
                        g, h = chunk(t1, half), chunk(t2, half)
                        dve.wait_ge(slot_done, slot + 1)
                        V.tensor_tensor(out=g, in0=bank[2 * half][:, :], in1=r[:, :],
                                        op=ALU.mult).then_inc(gate_ready, 1)
                        dve.wait_ge(slot_done, slot + 2)
                        V.tensor_tensor(out=h, in0=bank[2 * half + 1][:, :], in1=r[:, :],
                                        op=ALU.mult).then_inc(gu_free, 1)
                        dve.wait_ge(gu_free, done + 2)
                        dve.wait_ge(silu_ready, done)
                        V.tensor_tensor(out=h, in0=g, in1=h, op=ALU.mult).then_inc(prod_ready, 1)
                        dve.wait_ge(a_hi_ready, done)
                        V.tensor_tensor(out=a_lo[:, ds(f * T + half * T, T)], in0=h,
                                        in1=a_hi[:, ds(f * T + half * T, T)].bitcast(f32),
                                        op=ALU.subtract).then_inc(a_lo_ready, 1)
                update(l, ph, ACC_BASE[2 * e] + ACC * (FC - 1), FFN_BASE[e] + FFN_SLOTS, 0.5)

            def mix(l):
                prepare(l, 1, G_MIX)
                invert(l, 1)

                def evacuate(j, slot, out_, in_, rr):
                    dve.wait_ge(slot_done, l * SLOTS + (RING + slot + 1))
                    V.tensor_tensor(out=out_, in0=in_, in1=rr, op=ALU.mult).then_inc(proj_ready, 1)

                evacuate(0, MIX_BASE["iq"], chunk(iq, 0), bank[0][:, :], r[:, :])
                evacuate(1, MIX_BASE["iq"] + 1, chunk(iq, 1), bank[1][:, :], r[:, :])
                evacuate(2, MIX_BASE["ik"], ik[:, :], bank[2][:, :], r[:, :])
                dve.wait_ge(msq_ready, l + 1)
                for half in (4 * MEM, 2 * MEM):
                    link(l, V.tensor_tensor(out=sq[:, 0:half], in0=sq[:, 0:half],
                                            in1=sq[:, half:2 * half], op=ALU.add))
                V.tensor_tensor(out=sq[:, 0:MEM], in0=sq[:, 0:MEM], in1=sq[:, MEM:2 * MEM],
                                op=ALU.add).then_inc(mssq_ready, 1)
                dve.wait_ge(m_hi_ready, (l + 1) * DC)
                for j in range(DC):
                    s = slice(j * MEM, (j + 1) * MEM)
                    last = V.scalar_tensor_tensor(out=m_lo[:, s], in0=mem[:, s],
                                                  scalar=par[:, ds(l * PARAMS + (G_MEM + j), 1)],
                                                  in1=m_hi[:, s].bitcast(f32), op0=ALU.mult,
                                                  op1=ALU.subtract)
                last.then_inc(m_lo_ready, 1)
                evacuate(3, MIX_BASE["iw"], iw[0:4, :], bank[3][0:4, :], r[0:4, :])
                dve.wait_ge(cols_done, l + 1)
                V.tensor_copy(cols[:, :], bank[3][:, 0:TT + 4 * TT]).then_inc(cols_ready, 1)
                dve.wait_ge(cols_ready, l + 1)

                n = 0
                for i in range(1, TT):
                    s = score[:, score_at[i]:score_at[i] + (i + 1) * P]
                    for h in range(IDX_HEADS):
                        dve.wait_ge(relu_ready, l * 12 + (n + 1))
                        c = TT + 4 * i + h
                        before = con(C_CAUSAL + T - (i + 1) * P, (i + 1) * P) if h == 0 else s
                        V.scalar_tensor_tensor(out=s, in0=chunk(t2, n % 2, T, (i + 1) * P),
                                               scalar=cols[:, c:c + 1], in1=before, op0=ALU.mult,
                                               op1=ALU.add).then_inc(acc_score, 1)
                        n += 1
                        wait_apart(dve, acc_score, l * 12 + n)

                def take_largest(i):
                    s = score[:, score_at[i]:score_at[i] + (i + 1) * P]
                    start = links[0]
                    with dve.Fori(0, ROUNDS_PER_STEP) as q:
                        now = l * DVE_CHAIN + q * 2 + start
                        V.max(top8[:, :], s).then_inc(dve_chain, 1)
                        wait_apart(dve, dve_chain, now + 1)
                        V.match_replace(s, top8[:, :], s, TAKEN).then_inc(dve_chain, 1)
                        dve.wait_ge(dve_chain, now + 2)
                    links[0] += 2 * ROUNDS_PER_STEP

                steps = [i for i in range(1, TT) for _ in range(ROUNDS // ROUNDS_PER_STEP)]
                take_largest(steps.pop(0))
                take_largest(steps.pop(0))
                dve.wait_ge(mrms_ready, l + 1)
                V.reciprocal(rmem[:, :], rmem[:, :]).then_inc(rmem_ready, 1)
                dve.wait_ge(rmem_ready, l + 1)
                for j in range(ZT + 1):
                    tile = ORDER[j]
                    if tile == "mk":
                        dve.wait_ge(slot_done, l * SLOTS + (RING + MIX_BASE["mk"] + 2))
                        for i in range(2):
                            last = V.tensor_tensor(out=chunk(mk, i, MEM), in0=chunk(bank[4], i, MEM),
                                                   in1=rmem[:, :], op=ALU.mult)
                        last.then_inc(proj_ready, 1)
                    else:
                        name, i = ("aq", "ak", "mq")[tile // 4], tile % 4
                        evacuate(4 + j, MIX_BASE[name] + i, chunk(z, tile), bank[tile % 4][:, :],
                                 r[:, :])
                    if steps:
                        take_largest(steps.pop(0))
                assert not steps
                for i in range(2):
                    evacuate(15 + i, MIX_BASE["pu"] + i,
                             u[:, i * (PAD + T) + PAD:(i + 1) * (PAD + T)], bank[2 + i][:, :], r[:, :])
                V.tensor_scalar(score[:, :], score[:, :], TAKEN, NEG, ALU.not_equal,
                                ALU.mult).then_inc(bias_ready, 1)
                dve.wait_ge(bias_ready, l + 1)
                dve.wait_ge(hrms_ready, l + 1)
                V.reciprocal(hrms[:, :], hrms[:, :]).then_inc(hinv_ready, 1)
                dve.wait_ge(mcols_done, l + 1)
                V.tensor_copy(rmem_col[:, :], bank[7][:, 0:MT]).then_inc(mcols_ready, 1)

                gains = [G_Q] * 4 + [G_K] * 4 + [G_MQ] * 2 + [G_MK] * 2
                for j in range(NORMED):
                    dve.wait_ge(spread_done, l * NORMED + (j + 1))
                    t = chunk(z, j) if j < ZT else chunk(mk, j - ZT, MEM)
                    V.scalar_tensor_tensor(out=t, in0=t, scalar=par[:, ds(l * PARAMS + gains[j], 1)],
                                           in1=bank[j % 3][:, 0:T if j < ZT else MEM], op0=ALU.mult,
                                           op1=ALU.mult).then_inc(zn_ready, 1)

                def pool_lo():
                    for i in range(2):
                        dve.wait_ge(ypool_hi, l * 2 + (i + 1))
                        V.scalar_tensor_tensor(out=chunk(y_lo, 4 + i), in0=bank[6 + i][:, :],
                                               scalar=par[:, ds(l * PARAMS + (G_POOL + i), 1)],
                                               in1=chunk(y_hi, 4 + i).bitcast(f32), op0=ALU.mult,
                                               op1=ALU.subtract).then_inc(ypool_lo, 1)

                def mask_and_max(n):
                    i, h, is_mem, blocks = unit(n)
                    if is_mem:
                        bias = con(C_CAUSAL, MEM)
                    elif i == 0:
                        bias = con(C_CAUSAL + T - P, P)
                    else:
                        bias = score[:, score_at[i]:score_at[i] + blocks * P]
                    if n >= 2:
                        dve.wait_ge(p_ready, l * UNITS + (n - 1))
                    wait_apart(dve, logit_done, l * UNITS + (n + 1))
                    V.tensor_tensor_reduce(out=chunk(t2, n % 2, T, blocks * P),
                                           in0=bank[n % 2][:, 0:blocks * P], in1=bias, scale=1.0,
                                           scalar=TAKEN, op0=ALU.add, op1=ALU.max,
                                           accum_out=rowmax[:, n:n + 1]).then_inc(lm_ready, 1)
                    dve.wait_ge(lm_ready, l * UNITS + (n + 1))
                    V.tensor_scalar(negmax[:, n:n + 1], rowmax[:, n:n + 1], -HD ** -0.5, None,
                                    ALU.mult).then_inc(nm_ready, 1)

                def finish(g):
                    i, is_mem = divmod(g, 2)
                    end = group_end(g)
                    n = MEM_HEADS if is_mem else HEADS
                    dve.wait_ge(pv_done, l * UNITS + end)
                    if g >= 2:
                        dve.wait_ge(ot_done, l * 2 * TT + (g - 1))
                    link(l, V.reciprocal(rinv[:, end - n:end], rowsum[:, end - n:end]))
                    o = o_sb[:, is_mem * T:is_mem * T + n * HD].rearrange("p (h d) -> p h d", d=HD)
                    ps = bank[4 + is_mem][:, 0:n * HD].rearrange("p (h d) -> p h d", d=HD)
                    ri = rinv[:, end - n:end].rearrange("p (h d) -> p h d", d=1).broadcast_to([P, n, HD])
                    V.tensor_tensor(out=o, in0=ps, in1=ri, op=ALU.mult).then_inc(o_ready, 1)

                def split_y(g):
                    i, is_mem = divmod(g, 2)
                    n = 2 if is_mem else 4
                    lo, hi = (t[:, (6 if is_mem else 0) * T:(8 if is_mem else 4) * T]
                              .rearrange("p (c t) -> p c t", t=T)[:, :, i * P:(i + 1) * P]
                              for t in (y_lo, y_hi))
                    dve.wait_ge(yt_hi, l * 2 * TT + (g + 1))
                    V.tensor_tensor(out=lo, in0=bank[6 + is_mem][:, 0:n * P]
                                    .rearrange("p (c t) -> p c t", t=P),
                                    in1=hi.bitcast(f32), op=ALU.subtract).then_inc(yt_lo, 1)

                for n in range(UNITS + 4):
                    if n < UNITS:
                        mask_and_max(n)
                    if n == POOL_UNIT + 1:
                        pool_lo()
                    if n - 2 in group_after:
                        finish(group_after[n - 2])
                    if n - 4 + 1 in group_after:
                        split_y(group_after[n - 4 + 1])
                update(l, 1, ACC_BASE[1] + ACC * (DC - 1), MIX_BASE["out"] + DC, 1.0)

            dve.wait_ge(params_loaded, 16)
            for q in range(X_PARTS):
                dve.wait_ge(x_loaded[q], 16)
                dve.sem_inc(x_new, DC // X_PARTS)
            dve.sem_inc(gu_free, 2)
            dve.wait_ge(consts_loaded, 16)
            with dve.Fori(0, LAYERS) as l:
                ffn(l, 0)
                mix(l)
                ffn(l, 1)
            assert links[0] == DVE_CHAIN, links[0]


def _constants():
    import numpy as np

    c = np.zeros((P, CONSTS), np.float32)
    p = np.arange(P)
    c[:, C_ID:C_ID + P] = np.eye(P)
    c[:, C_ONES:C_ONES + P] = 1
    c[:, C_BLOCK:C_BLOCK + P] = p[:, None] // HD == p[None, :] // HD
    c[:, C_CAUSAL + T - P:C_CAUSAL + T] = np.where(p[None, :] <= p[:, None], 0, NEG)
    for j in range(NORMED):
        for half in range(2):
            row = 2 * j + half
            c[half * HD:(half + 1) * HD, C_SEL + j * NROW + row] = 1
            c[row, C_SPREAD + j * P + half * HD:C_SPREAD + j * P + (half + 1) * HD] = 1
    for i in range(2):
        for half in range(2):
            w = WINDOWS[2 * i + half]
            s = slice(half * HD, (half + 1) * HD)
            c[s, C_INV + 16 * i:C_INV + 16 * (i + 1)] = 1 / np.minimum(np.arange(16) + 1, w)
            c[s, C_INVW + i] = 1 / w
    c[:, C_EPS] = EPS
    return c


def _by_output(w, n):
    return w.reshape(DC, P, n, P).transpose(2, 1, 0, 3).reshape(n, P, SLOT)


def _weight_stream(a, l):
    import numpy as np

    def ffn(gate, up, down):
        gu = np.stack([_by_output(gate, FC), _by_output(up, FC)], 1).reshape(2 * FC, P, SLOT)
        return [gu, down.reshape(FC, P, SLOT)]

    def by_tokens(w, chunks):
        return w.reshape(DC // chunks, chunks, P, -1).transpose(0, 2, 1, 3).reshape(-1, P, SLOT)

    w = a["w_in"][l]
    at = np.cumsum([0, 512, 512, 512, 256, 64, 4, 256, 256])
    aq, ak, av, iq, ik, iw, pu, mq = (w[:, at[i]:at[i + 1]] for i in range(8))
    kv = a["w_mem_kv"][l]
    iw = np.concatenate([iw, np.zeros((D, P - 4), iw.dtype)], 1)
    parts = ffn(a["ffn1_gate"][l], a["ffn1_up"][l], a["ffn1_down"][l])
    parts += [_by_output(iq, 2), _by_output(np.concatenate([ik, ik], 1), 1), _by_output(iw, 1),
              by_tokens(av, 2), _by_output(aq, 4), _by_output(ak, 4), _by_output(kv[:, :256], 2),
              _by_output(mq, 2), _by_output(pu, 2), by_tokens(kv[:, 256:], 4),
              a["w_out"][l].reshape(DC, P, SLOT)]
    parts += ffn(a["ffn2_gate"][l], a["ffn2_up"][l], a["ffn2_down"][l])
    return parts


def kernel(**inputs):
    import numpy as np
    import concourse.bacc as bacc
    from concourse.bass_utils import run_bass_kernel_spmd

    a = {k: np.asarray(v) for k, v in inputs.items()}

    def transposed(m):
        return m.reshape(-1, DC, P).transpose(2, 1, 0).reshape(P, -1)

    params = []
    pool_w = np.zeros((LAYERS, P, 2 * P), np.float32)
    for l in range(LAYERS):
        for name in ("ffn1_norm", "mix_norm", "ffn2_norm", "mem_norm"):
            params.append(a[name][l].reshape(DC, P).T)
        for name in ("q_norm", "k_norm", "mq_norm", "mk_norm"):
            params.append(np.concatenate([a[name][l]] * 2)[:, None])
        params.append(a["pool_scale"][l].reshape(2, P).T)
        for g in range(4):
            i, half = divmod(g, 2)
            pool_w[l, half * HD:(half + 1) * HD, i * P + half * HD:i * P + (half + 1) * HD] = a["w_pool"][l, g]
    data = {
        "x_t": transposed(a["x"][0]),
        "mem_t": transposed(a["mem"][0]),
        "weights": np.concatenate([p for l in range(LAYERS) for p in _weight_stream(a, l)]
                                  + [np.zeros((RING, P, SLOT), np.float32)], 0),
        "pool_w": pool_w,
        "params": np.concatenate(params, 1),
        "consts": _constants(),
    }
    nc = bacc.Bacc("TRN2", target_bir_lowering=False, num_devices=1)
    arrays, args = {}, []
    for name, v in data.items():
        arrays[name] = np.ascontiguousarray(v)
        args.append(nc.dram_tensor(name, arrays[name].shape, mybir.dt.from_np(arrays[name].dtype),
                                   kind="ExternalInput").ap())
    out = nc.dram_tensor("out_t", (P, DC * T), mybir.dt.float32, kind="ExternalOutput").ap()
    build(nc, *args, out)
    res = run_bass_kernel_spmd(nc, [arrays], core_ids=[0])
    got = res.results[0]["out_t"].reshape(P, DC, T).transpose(2, 1, 0).reshape(1, T, D)
    return np.ascontiguousarray(got)
```

```python
import concourse.bass as bass
from concourse import mybir

P = 128
D = 1024
T = 512
LAYERS = 2
HD = 64
HEADS = 8
IDX_HEADS = 4
MEM_HEADS = 4
MEM = 256
FF = 2816
TOPK = min(256, T // 4)
WINDOWS = (2, 4, 8, 16)
EPS = 1e-6

DC = D // P
TT = T // P
MT = MEM // P
FC = FF // P
SLOT = DC * P
RING = 4

MIX_SLOTS = (("iq", 2), ("ik", 1), ("iw", 1), ("av", 4), ("aq", 4), ("ak", 4), ("mq", 2), ("pu", 2),
             ("mk", 2), ("mv", 2), ("out", 8))
FFN_SLOTS = 2 * FC + FC
MIX_BASE = {}
_at = FFN_SLOTS
for _name, _n in MIX_SLOTS:
    MIX_BASE[_name] = _at
    _at += _n
FFN_BASE = (0, _at)
SLOTS = _at + FFN_SLOTS
assert SLOTS % RING == 0

G_FFN1, G_MIX, G_FFN2, G_MEM = 0, DC, 2 * DC, 3 * DC
G_Q, G_K, G_MQ, G_MK, G_POOL = (4 * DC + i for i in range(5))
PARAMS = 4 * DC + 4 + 2

ZT = HEADS // 2 * 2 + MEM_HEADS // 2
NORMED = ZT + MEM_HEADS // 2
Z_ROWS = 2 * ZT
MK_ROW = 32
MK_ROWS = 2 * (NORMED - ZT)
NROW = MK_ROW + MK_ROWS
C_ID = 0
C_ONES = C_ID + P
C_CAUSAL = C_ONES + P
C_SEL = C_CAUSAL + T
C_SEL_MK = C_SEL + ZT * Z_ROWS
C_INV = C_SEL_MK + (NORMED - ZT) * MK_ROWS
C_INVW = C_INV + 2 * 16
C_EPS = C_INVW + 2
CONSTS = C_EPS + 1

X_PARTS = 4
NEG = -1e30
TAKEN = -3e38
ROUNDS = TOPK // 8
FIRST_ROUNDS = ROUNDS - ZT
UNITS_PER_TILE = HEADS + MEM_HEADS
UNITS = TT * UNITS_PER_TILE
POOL_UNITS = (29, 31)
LAG = 3
OUT_ROUND_UNITS = (9, 11, 21, 23)
OUT_ORDER = [4, 5, 0, 1, 2, 3, 6, 7]
FILL = {UNITS - 1: 0, UNITS: 1, UNITS + 1: 4, UNITS + LAG - 1: 2, UNITS + LAG: 3}
ORDER = [0, 1, 2, 3, 4, 5, 6, 7, 8, 9, "mk"]
NORM_ORDER = [0, 4, 1, 5, 2, 6, 3, 7, 8, 9, 10, 11]
NORM_EARLY = 8

POOL_CHAIN = 14
ROUND_CHAIN = 2 * (TT - 1)
DVE_CHAIN = 104


def build(nc, x_t, mem_t, weights, pool_w, params, consts, spreads, out):
    f32, f32r = mybir.dt.float32, mybir.dt.float32r
    ALU, ACT = mybir.AluOpType, mybir.ActivationFunctionType
    ds = bass.ds

    base = -(-nc.sbuf_base // 64) * 64
    tile_b = T * 4

    def place(name, cols, at, dt=f32, parts=P):
        return nc.alloc_sbuf_tensor_at(name, [parts, cols], dt, offset=at)

    cursor = [base]

    def new(name, cols, dt=f32, parts=P):
        at = cursor[0]
        cursor[0] += -(-cols * 4 // 64) * 64
        return place(name, cols, at, dt, parts)

    x = new("x", DC * T)
    h_hi = new("h_hi", DC * T, f32r)
    h_lo = new("h_lo", DC * T, f32r)
    raw = new("raw", RING * SLOT)
    w_hi = new("w_hi", RING * SLOT, f32r)
    w_lo = new("w_lo", RING * SLOT, f32r)
    a_hi_at = cursor[0]
    a_hi = new("a_hi", FC * T, f32r)
    a_lo_at = cursor[0]
    a_lo = new("a_lo", FC * T, f32r)
    r = new("r", T)
    t1 = new("t1", 2 * T)
    t2 = new("t2", 2 * T)
    const = new("const", CONSTS)
    par = new("par", LAYERS * PARAMS)
    wpool = new("wpool", 2 * P)
    cols = new("cols", TT + TT * IDX_HEADS)
    rmem_col = new("rmem_col", MT)
    spread = new("spread", NORMED * P, f32r, NROW)
    assert cursor[0] <= nc.sbuf_usable_end, cursor[0]
    y_hi, y_lo = a_hi, a_lo
    m_hi = a_hi[:, 8 * T:8 * T + DC * MEM]
    m_lo = a_lo[:, 8 * T:8 * T + DC * MEM]
    z = place("z", ZT * T, a_hi_at + 12 * tile_b)
    mem = place("mem", DC * MEM, a_hi_at)
    u = place("u", 2 * T, a_hi_at + 4 * tile_b)
    wa = place("wa", T, a_hi_at + 11 * tile_b)
    wb = place("wb", T, a_lo_at + 11 * tile_b)
    idx = place("idx", 3 * T, a_lo_at)
    iw = place("iw", T, a_lo_at + 3 * tile_b)
    idx_hi = place("idx_hi", 3 * T, a_hi_at + 12 * tile_b, f32r)
    idx_lo = place("idx_lo", 3 * T, a_hi_at + 15 * tile_b, f32r)
    hrms = place("hrms", T, a_lo_at, parts=NROW)
    hr_hi, hr_lo = (a_lo[0:NROW, i * T:(i + 1) * T] for i in (6, 7))
    spread_in = place("spread_in", NORMED * P, a_hi_at + 4 * tile_b, parts=NROW)
    v = place("v", TT * T, a_lo_at + 12 * tile_b)
    mk = place("mk", 2 * MEM, a_lo_at + 16 * tile_b)
    mv = place("mv", MT * MEM, a_lo_at + 17 * tile_b)
    score_at = [0, 0, 2 * P, 5 * P]
    score = place("score", 9 * P, a_lo_at + 18 * tile_b)
    small = a_lo_at + 21 * tile_b
    rmem = place("rmem", MEM, small)
    negmax, rowsum, rinv = (
        place(name, UNITS, small + (MEM + i * UNITS) * 4)
        for i, name in enumerate(("negmax", "rowsum", "rinv")))
    top8 = place("top8", 8 * TT, small + (MEM + 3 * UNITS) * 4)
    sq = place("sq", DC * T, a_lo_at + 14 * tile_b)
    zn_hi = [h_hi[:, j * T:(j + 1) * T] for j in range(8)] + \
            [a_hi[:, j * T:(j + 1) * T] for j in (8, 9)] + \
            [a_hi[:, 10 * T + i * MEM:10 * T + (i + 1) * MEM] for i in range(2)]
    zn_lo = [h_lo[:, j * T:(j + 1) * T] for j in range(8)] + \
            [a_lo[:, j * T:(j + 1) * T] for j in (8, 9)] + \
            [a_lo[:, 10 * T + i * MEM:10 * T + (i + 1) * MEM] for i in range(2)]
    pt = [place(f"pt{i}", T, a_hi_at + (12 + j) * tile_b) for i, j in enumerate((0, 4))]
    prob = [t1[:, 0:T], t1[:, T:2 * T]] + \
           [place(f"prob{j}", T, a_hi_at + (12 + j) * tile_b)[:, :] for j in (1, 5)]
    rt = place("rt", T, a_hi_at + (12 + 2) * tile_b)
    yt = place("yt", T, a_hi_at + (12 + 3) * tile_b)

    bank = [nc.alloc_psum_tensor(f"bank{i}", [P, 512], f32) for i in range(8)]
    logit_bank = [bank[0], bank[1], bank[4]]

    def chunk(t, j, n=T, size=None):
        return t[:, j * n:j * n + (size or n)]

    def con(at, n=1, parts=P):
        return const[0:parts, at:at + n]

    def sem(name):
        return nc.alloc_semaphore(name)

    w_loaded = [sem(f"w_loaded{i}") for i in range(RING)]
    w_hi_done = sem("w_hi_done")
    w_ready = sem("w_ready")
    slot_done = sem("slot_done")
    acc_done = sem("acc_done")
    params_loaded = sem("params_loaded")
    consts_loaded = sem("consts_loaded")
    x_loaded = [sem(f"x_loaded{q}") for q in range(X_PARTS)]
    mem_loaded = sem("mem_loaded")
    pool_w_loaded = sem("pool_w_loaded")
    out_stored = sem("out_stored")
    x_new = sem("x_new")
    hi_ready = sem("hi_ready")
    lo_ready = sem("lo_ready")
    sq_ready = sem("sq_ready")
    ssq_ready = sem("ssq_ready")
    sum_done = sem("sum_done")
    rms_ready = sem("rms_ready")
    r_ready = sem("r_ready")
    gate_ready = sem("gate_ready")
    gu_free = sem("gu_free")
    silu_ready = sem("silu_ready")
    prod_ready = sem("prod_ready")
    a_hi_ready = sem("a_hi_ready")
    a_lo_ready = sem("a_lo_ready")
    proj_ready = sem("proj_ready")
    msq_ready = sem("msq_ready")
    mssq_ready = sem("mssq_ready")
    msum_done = sem("msum_done")
    mrms_ready = sem("mrms_ready")
    rmem_ready = sem("rmem_ready")
    m_hi_ready = sem("m_hi_ready")
    m_lo_ready = sem("m_lo_ready")
    cols_done = sem("cols_done")
    cols_ready = sem("cols_ready")
    mcols_done = sem("mcols_done")
    mcols_ready = sem("mcols_ready")
    v_ready = sem("v_ready")
    mv_ready = sem("mv_ready")
    idx_hi_ready = sem("idx_hi_ready")
    idx_lo_ready = sem("idx_lo_ready")
    dots_done = sem("dots_done")
    relu_ready = sem("relu_ready")
    acc_score = sem("acc_score")
    bias_ready = sem("bias_ready")
    zsq_ready = sem("zsq_ready")
    zsum_done = sem("zsum_done")
    hrms_ready = sem("hrms_ready")
    hinv_ready = sem("hinv_ready")
    spread_loaded = sem("spread_loaded")
    spread_ready = sem("spread_ready")
    hr_hi_ready = sem("hr_hi_ready")
    hr_lo_ready = sem("hr_lo_ready")
    zhi_ready = sem("zhi_ready")
    zlo_ready = sem("zlo_ready")
    spread_done = sem("spread_done")
    zn_ready = sem("zn_ready")
    pooled_ready = sem("pooled_ready")
    pool_done = sem("pool_done")
    ypool_hi = sem("ypool_hi")
    ypool_lo = sem("ypool_lo")
    logit_done = sem("logit_done")
    lm_ready = sem("lm_ready")
    p_ready = sem("p_ready")
    rinv_ready = sem("rinv_ready")
    rt_done = sem("rt_done")
    rt_ready = sem("rt_ready")
    ptp_done = sem("ptp_done")
    pt_ready = [sem("pt_even_ready"), sem("pt_odd_ready")]
    pv_done = sem("pv_done")
    y_ready = sem("y_ready")
    yt_hi = sem("yt_hi")
    yt_lo = sem("yt_lo")
    dve_chain = sem("dve_chain")
    pool_chain = sem("pool_chain")

    ACC = 7
    ACC_BASE = (0, FC * ACC, FC * ACC + 8 * ACC)
    ACC_LAYER = ACC * (2 * FC + 8)

    def unit(n):
        s, h = divmod(n, UNITS_PER_TILE)
        i = TT - 1 - s
        is_mem = h >= HEADS
        return i, (h - HEADS if is_mem else h), is_mem, (MT if is_mem else i + 1)

    def group_end(g):
        s, is_mem = divmod(g, 2)
        return s * UNITS_PER_TILE + (UNITS_PER_TILE if is_mem else HEADS)

    group_after = {group_end(g): g for g in range(2 * TT)}

    def y_bank(g):
        return bank[6 if g % 2 else 5]

    def spread_bank(k):
        return bank[k % 3 if k < NORM_EARLY else (7, 6)[k % 2]]

    def query_tile(g):
        return TT - 1 - g // 2

    passed = sem("passed")

    def wait_apart(eng, s, value):
        eng.wait_ge(s, value)
        eng.sem_inc(passed, 1)

    def on_vector(n):
        return n % 2 == 1

    def group_start(g):
        return group_end(g) - (MEM_HEADS if g % 2 else HEADS)

    def copy_pt(eng, copy, l, n):
        blocks = unit(n)[3]
        eng.wait_ge(ptp_done, l * UNITS + (n + 1))
        if n >= 2:
            eng.wait_ge(pv_done, l * UNITS + (n - 1))
        copy(pt[n % 2][:, 0:blocks * P], bank[2 + n % 2][:, 0:blocks * P])\
            .then_inc(pt_ready[n % 2], 1)

    def head_rms(j):
        return (slice(0, Z_ROWS), T) if j < ZT else (slice(MK_ROW, NROW), MEM)

    with nc.Block() as block:

        @block.sync
        def _(sp):
            def load(n, pos, first=False):
                if not first:
                    sp.wait_ge(w_ready, n + (1 - RING))
                src = weights[ds(n, 1), :, :].rearrange("a p n -> (a p) n")
                sp.dma_start(raw[:, pos * SLOT:(pos + 1) * SLOT], src).then_inc(w_loaded[pos], 16)

            sp.dma_start(par[:, :], params[:, :]).then_inc(params_loaded, 16)
            for q in range(X_PARTS):
                s = slice(q * DC // X_PARTS * T, (q + 1) * DC // X_PARTS * T)
                sp.dma_start(x[:, s], x_t[:, s]).then_inc(x_loaded[q], 16)
                if q == 0:
                    load(0, 0, first=True)
            load(1, 1, first=True)
            sp.dma_start(const[:, :], consts[:, :]).then_inc(consts_loaded, 16)
            load(2, 2, first=True)
            load(3, 3, first=True)
            with sp.Fori(1, LAYERS * SLOTS // RING + 1) as i:
                for pos in range(RING):
                    load(i * RING + pos, pos)
            for pos in range(RING):
                sp.wait_ge(w_loaded[pos], 16 * (LAYERS * SLOTS // RING + 1))
            for j in range(DC):
                sp.wait_ge(x_new, 3 * DC * LAYERS + j + 1)
                sp.dma_start(out[:, j * T:(j + 1) * T], chunk(x, j)).then_inc(out_stored, 16)
            sp.wait_ge(out_stored, 16 * DC)

        @block.gpsimd
        def _(pool):
            G = nc.gpsimd
            steps = [0]

            def rest(l, n):
                pos = n[1] % RING
                s = slice(pos * SLOT, (pos + 1) * SLOT)
                pool.wait_ge(w_hi_done, l * SLOTS + n[0] + (n[1] + 1))
                G.tensor_tensor(out=w_lo[:, s], in0=raw[:, s], in1=w_hi[:, s].bitcast(f32),
                                op=ALU.subtract).then_inc(w_ready, 1)

            def step(l, ins):
                steps[0] += 1
                ins.then_inc(pool_chain, 1)
                pool.wait_ge(pool_chain, l * POOL_CHAIN + steps[0])

            def pooling(l):
                wait_apart(pool, proj_ready, l * 17 + 16)
                for i in range(2):
                    ui = chunk(u, i)

                    def shifted_sum(p0, dst, src, by):
                        G.tensor_tensor(out=dst[p0:P, by:T], in0=src[p0:P, by:T],
                                        in1=src[p0:P, 0:T - by], op=ALU.add)
                        step(l, G.tensor_copy(dst[p0:P, 0:by], src[p0:P, 0:by]))

                    shifted_sum(0, wa, ui, 1)
                    if i == 0:
                        shifted_sum(HD, wb, wa, 2)
                    else:
                        shifted_sum(0, wb, wa, 2)
                        shifted_sum(0, wa, wb, 4)
                        shifted_sum(HD, wb, wa, 8)
                    for half, w in enumerate((wa, wb)):
                        p = slice(half * HD, (half + 1) * HD)
                        G.tensor_tensor(out=w[p, 0:16], in0=w[p, 0:16],
                                        in1=const[p, C_INV + 16 * i:C_INV + 16 * (i + 1)], op=ALU.mult)
                        step(l, G.tensor_scalar(w[p, 16:T], w[p, 16:T],
                                                const[p, C_INVW + i:C_INVW + i + 1], None, ALU.mult))
                        step(l, G.tensor_tensor(out=ui[p, :], in0=w[p, :], in1=ui[p, :],
                                                op=ALU.subtract))
                    pool.sem_inc(pooled_ready, 1)

            ahead = MIX_BASE["out"]
            with pool.Fori(0, LAYERS) as l:
                with pool.Fori(0, ahead // RING) as i:
                    for pos in range(RING):
                        rest(l, (i * RING, pos))
                for n in range(ahead // RING * RING, ahead):
                    rest(l, (0, n))
                for k, j in enumerate(NORM_ORDER):
                    t = chunk(z, j) if j < ZT else chunk(mk, j - ZT, MEM)
                    pool.wait_ge(zhi_ready, l * NORMED + (k + 1))
                    G.tensor_tensor(out=zn_lo[j], in0=t, in1=zn_hi[j].bitcast(f32),
                                    op=ALU.subtract).then_inc(zlo_ready, 1)
                pooling(l)
                first = -(-(ahead + RING) // RING) * RING
                for n in range(ahead, first):
                    rest(l, (0, n))
                with pool.Fori(0, (SLOTS - first) // RING) as i:
                    for pos in range(RING):
                        rest(l, (i * RING, first + pos))
            assert steps[0] == POOL_CHAIN, steps[0]

        @block.tensor
        def _(pe):
            def mm(out_, lhsT, rhs, start=True, stop=True):
                return nc.tensor.matmul(out_, lhsT, rhs, start=start, stop=stop, skip_group_check=True)

            def passes(out_, w, act, start, stop):
                (whi, wlo), (ahi, alo) = w, act
                mm(out_, whi, ahi, start, False)
                mm(out_, whi, alo, False, False)
                return mm(out_, wlo, ahi, False, stop)

            def weight(pos, at, n=P):
                s = slice(pos * SLOT + at, pos * SLOT + at + n)
                return w_hi[:, s], w_lo[:, s]

            def pair(hi, lo, at, n=T):
                return hi[:, at:at + n], lo[:, at:at + n]

            def project_first(l, ph, n):
                def with_hi(i, k, part):
                    mm(bank[i][:, :], weight((n + i) % RING, k * P)[part], chunk(h_hi, k),
                       part == 0 and k == 0, False)

                def rounded(k):
                    pe.wait_ge(hi_ready, (l * 3 + ph) * DC + (k + 1))

                if ph == 0:
                    pe.wait_ge(w_hi_done, l * SLOTS + (n + 1))
                    for k in range(DC):
                        rounded(k)
                        with_hi(0, k, 0)
                        if k == 0:
                            pe.wait_ge(w_ready, l * SLOTS + (n + 1))
                        with_hi(0, k, 1)
                    pe.wait_ge(w_ready, l * SLOTS + (n + 2))
                    for k in range(DC):
                        for part in range(2):
                            with_hi(1, k, part)
                else:
                    pe.wait_ge(w_ready, l * SLOTS + (n + 2))
                    for k in range(DC):
                        rounded(max(k, 1))
                        for i in range(2):
                            for part in range(2):
                                with_hi(i, k, part)
                for i in range(2):
                    for k in range(DC):
                        if i == 0:
                            pe.wait_ge(lo_ready, (l * 3 + ph) * DC + (k + 1))
                        last = mm(bank[i][:, :], weight((n + i) % RING, k * P)[0], chunk(h_lo, k),
                                  False, k == DC - 1)
                    last.then_inc(slot_done, 1)

            def project(l, n, to, hi, lo, width=T):
                pe.wait_ge(w_ready, l * SLOTS + (n + 1))
                for k in range(DC):
                    last = passes(to, weight(n % RING, k * P), pair(hi, lo, k * width, width),
                                  k == 0, k == DC - 1)
                last.then_inc(slot_done, 1)

            def token_sums(l, ph):
                pe.wait_ge(consts_loaded, 16)
                pe.wait_ge(ssq_ready, l * 3 + (ph + 1))
                mm(bank[4][:, :], con(C_ONES, P), chunk(sq, 0)).then_inc(sum_done, 1)

            def accumulate(pos, hi, lo, start, stop, banks=range(DC), at=0):
                for i, j in enumerate(banks):
                    last = passes(bank[j][:, :], weight(pos, j * P), (hi, lo), start, stop)
                    if at + i < ACC:
                        last.then_inc(acc_done, 1)
                    else:
                        last.then_inc(slot_done, 1)

            def ffn(l, e):
                ph, ffn_at = 2 * e, FFN_BASE[e]
                def gate_up(f, half):
                    n = ffn_at + 2 * half
                    pe.wait_ge(gu_free, (l * 2 + e) * FC + (f + (half + 1)))
                    at = l * SLOTS + ffn_at + f * 2 + 2 * half
                    for up in range(2):
                        pos = (n + up) % RING
                        pe.wait_ge(w_ready, at + (up + 1))
                        for k in range(DC):
                            last = passes(bank[2 * half + up][:, :], weight(pos, k * P),
                                          pair(h_hi, h_lo, k * T), k == 0, k == DC - 1)
                        last.then_inc(slot_done, 1)

                pe.wait_ge(gu_free, (l * 2 + e) * FC + 1)
                project_first(l, ph, ffn_at)
                token_sums(l, ph)
                gate_up(0, 1)
                with pe.Fori(1, FC // 2) as i:
                    gate_up(i * 2, 0)
                    gate_up(i * 2, 1)

                down_at = ffn_at + 2 * FC
                def down(f, off, start=False, stop=False, **part):
                    at = l * SLOTS + down_at + f + off
                    pe.wait_ge(w_ready, at + 1)
                    pe.wait_ge(a_lo_ready, (l * 2 + e) * FC + (f + (off + 1)))
                    fo = f * T + off * T
                    pos = (down_at + off + (f if isinstance(f, int) else 0)) % RING
                    accumulate(pos, a_hi[:, ds(fo, T)], a_lo[:, ds(fo, T)], start, stop, **part)

                pe.wait_ge(rms_ready, l * 3 + (ph + 1))
                down(0, 0, start=True, banks=range(4, DC))
                pe.wait_ge(gu_free, (l * 2 + e) * FC + (FC + 2))
                down(0, 0, start=True, banks=range(4), at=4)
                down(0, 1)
                with pe.Fori(0, (FC - 2) // RING - 1) as i:
                    for off in range(RING):
                        down(i * RING, 2 + off)
                for off in range(RING):
                    down(FC - RING, off, stop=off == RING - 1)

            def mix(l):
                def at(name, i=0):
                    return MIX_BASE[name] + i

                def heads_sum(j):
                    pe.wait_ge(zsq_ready, l * (ZT + 1) + (j + 1))
                    if ORDER[j] == "mk":
                        for i in range(2):
                            last = mm(bank[6][MK_ROW:NROW, 0:MEM],
                                      con(C_SEL_MK + i * MK_ROWS, MK_ROWS),
                                      t1[:, (j % 2) * T + i * MEM:(j % 2) * T + (i + 1) * MEM],
                                      i == 0, i == 1)
                    else:
                        last = mm(bank[6][0:Z_ROWS, :], con(C_SEL + ORDER[j] * Z_ROWS, Z_ROWS),
                                  chunk(t1, j % 2), j == 0, j == ZT - 1)
                    last.then_inc(zsum_done, 1)

                project_first(l, 1, at("iq"))
                token_sums(l, 1)
                project(l, at("ik"), bank[2][:, :], h_hi, h_lo)
                project(l, at("iw"), bank[3][:, :], h_hi, h_lo)
                pe.wait_ge(rms_ready, l * 3 + 2)

                def project_v(s):
                    n = at("av", s)
                    pe.wait_ge(w_ready, l * SLOTS + (n + 1))
                    for half in range(2):
                        k = 2 * s + half
                        whi, wlo = weight(n % RING, half * T, T)
                        for i in range(TT):
                            hhi, hlo = pair(h_hi, h_lo, k * T + i * P, P)
                            last = passes(bank[4 + i][:, :], (hhi, hlo), (whi, wlo),
                                          k == 0, k == DC - 1)
                    last.then_inc(slot_done, 1)

                project_v(0)
                project_v(1)
                pe.wait_ge(proj_ready, l * 17 + 4)
                for i in range(TT):
                    mm(bank[3][:, i:i + 1], r[0:1, i * P:(i + 1) * P], con(C_ONES, 1, 1))
                for i in range(TT):
                    last = mm(bank[3][:, TT + 4 * i:TT + 4 * i + 4], iw[0:4, i * P:(i + 1) * P],
                              con(C_ID, 4, 4))
                last.then_inc(cols_done, 1)
                n = 0
                pe.wait_ge(idx_lo_ready, (l + 1) * 3)
                for i in range(1, TT):
                    for h in range(IDX_HEADS):
                        if n >= 2:
                            pe.wait_ge(relu_ready, l * 12 + (n - 1))
                        p0 = HD * (h % 2)
                        at_q = (h // 2) * T + i * P
                        q = [t[p0:p0 + HD, at_q:at_q + P] for t in (idx_hi, idx_lo)]
                        k = [t[p0:p0 + HD, 2 * T:2 * T + (i + 1) * P] for t in (idx_hi, idx_lo)]
                        passes(bank[n % 2][:, 0:(i + 1) * P], q, k, True, True)\
                            .then_inc(dots_done, 1)
                        n += 1
                project_v(2)
                project_v(3)
                pe.wait_ge(mssq_ready, l + 1)
                mm(bank[2][:, 0:MEM], con(C_ONES, P), sq[:, 0:MEM]).then_inc(msum_done, 1)

                def project_z(t, name, i):
                    if t < 6:
                        pe.wait_ge(relu_ready, (l + 1) * 12)
                    elif t == 6:
                        pe.wait_ge(mrms_ready, l + 1)
                    elif t == 7:
                        pe.wait_ge(cols_ready, l + 1)
                    else:
                        pe.wait_ge(proj_ready, l * 17 + (t - 3))
                    project(l, at(name, i), bank[t % 4][:, :], h_hi, h_lo)

                for i in range(4):
                    project_z(4 + i, "aq", i)
                    if i >= 2:
                        heads_sum(i - 2)
                for i in range(4):
                    project_z(8 + i, "ak", i)
                    heads_sum(2 + i)
                pe.wait_ge(v_ready, (l + 1) * TT)
                pe.wait_ge(rmem_ready, l + 1)
                for i in range(MT):
                    last = mm(bank[7][:, i:i + 1], rmem[0:1, i * P:(i + 1) * P], con(C_ONES, 1, 1))
                last.then_inc(mcols_done, 1)
                project_z(12, "mq", 0)
                heads_sum(6)
                project_z(13, "mq", 1)
                heads_sum(7)
                project_z(14, "pu", 0)
                heads_sum(8)
                heads_sum(9)
                project_z(15, "pu", 1)

                def spread_rms(k):
                    j = NORM_ORDER[k]
                    if k == 0:
                        pe.wait_ge(spread_ready, l + 1)
                        pe.wait_ge(hr_lo_ready, l * 2 + 1)
                    if k < 3:
                        pe.wait_ge(proj_ready, l * 17 + (13 + k))
                    elif k < NORM_EARLY:
                        pe.wait_ge(zn_ready, l * NORMED + (k - 2))
                    elif k == NORM_EARLY:
                        pe.wait_ge(mcols_ready, l + 1)
                    elif k == NORM_EARLY + 1:
                        pe.wait_ge(hrms_ready, (l + 1) * 2)
                    else:
                        pe.wait_ge(zn_ready, l * NORMED + (k - 1))
                    if j == ZT:
                        pe.wait_ge(hr_lo_ready, l * 2 + 2)
                    rows, n = head_rms(j)
                    to = spread_bank(k)[:, 0:n]
                    mm(to, spread[rows, j * P:(j + 1) * P], hr_hi[rows, 0:n], True, False)
                    mm(to, spread[rows, j * P:(j + 1) * P], hr_lo[rows, 0:n], False, True)\
                        .then_inc(spread_done, 1)

                spread_rms(0)
                spread_rms(1)
                pe.wait_ge(m_lo_ready, l + 1)
                project(l, at("mk", 0), bank[4][:, 0:MEM], m_hi, m_lo, MEM)
                spread_rms(2)
                spread_rms(3)
                spread_rms(4)
                project(l, at("mk", 1), bank[4][:, MEM:2 * MEM], m_hi, m_lo, MEM)
                spread_rms(5)
                spread_rms(6)
                pe.wait_ge(w_ready, l * SLOTS + (at("mv") + 2))
                for i in range(MT):
                    for k in range(DC):
                        s, q = divmod(k, 4)
                        last = passes(bank[5][:, i * MEM:(i + 1) * MEM],
                                      pair(m_hi, m_lo, k * MEM + i * P, P),
                                      weight(at("mv", s) % RING, q * MEM, MEM), k == 0, k == DC - 1)
                        if i == MT - 1 and q == 3:
                            last.then_inc(slot_done, 1)
                    if i == 0:
                        spread_rms(7)
                        heads_sum(10)

                pools_after = max(g for n, g in group_after.items() if n + 2 < POOL_UNITS[0])

                def pool_map(i):
                    pe.wait_ge(pool_w_loaded, (l + 1) * 16)
                    pe.wait_ge(pooled_ready, l * 2 + (i + 1))
                    if i == 0:
                        pe.wait_ge(rt_ready, l * 2 * TT + (pools_after + 1))
                    else:
                        pe.wait_ge(y_ready, l * 2 * TT + (pools_after + 1))
                    mm(bank[7 - i][:, :], chunk(wpool, i, P),
                       chunk(u, i)).then_inc(pool_done, 1)

                pe.wait_ge(zn_ready, l * NORMED + NORM_EARLY)
                pe.wait_ge(proj_ready, (l + 1) * 17)

                def out_chunk(k, banks=range(DC), done=0):
                    n, c = at("out", k), OUT_ORDER[k]
                    if done < ACC:
                        pe.wait_ge(w_ready, l * SLOTS + (n + 1))
                    accumulate(n % RING, chunk(y_hi, c), chunk(y_lo, c), k == 0, k == DC - 1,
                               banks, done)

                def fill(b):
                    if b == 0:
                        pe.wait_ge(ypool_lo, (l + 1) * 2)
                    if b in (0, 1, 4):
                        pe.wait_ge(lm_ready, l * UNITS + (UNITS - 2 + (0, 1, 4).index(b)))
                    else:
                        pe.wait_ge(pt_ready[b % 2], (l + 1) * (UNITS // 2))
                    at_fill = list(FILL.values()).index(b)
                    out_chunk(0, [b], at_fill)
                    out_chunk(1, [b], at_fill)

                def logits(n):
                    i, h, is_mem, blocks = unit(n)
                    if n >= 3:
                        pe.wait_ge(lm_ready, l * UNITS + (n - 2))
                    p0, j = HD * (h % 2), h // 2
                    qt, kt = (8 + j, 10 + j) if is_mem else (j, 4 + j)
                    if i == TT - 1:
                        pe.wait_ge(zlo_ready, l * NORMED + (NORM_ORDER.index(kt) + 1))
                    q = [t[qt][p0:p0 + HD, i * P:(i + 1) * P] for t in (zn_hi, zn_lo)]
                    k = [t[kt][p0:p0 + HD, 0:blocks * P] for t in (zn_hi, zn_lo)]
                    passes(logit_bank[n % 3][:, 0:blocks * P], q, k, True, True)\
                        .then_inc(logit_done, 1)

                def transpose_p(n):
                    i, h, is_mem, blocks = unit(n)
                    pe.wait_ge(p_ready, l * UNITS + (n + 1))
                    if n >= 2:
                        pe.wait_ge(pt_ready[n % 2], l * (UNITS // 2) + n // 2)
                    for b in range(blocks):
                        last = nc.tensor.transpose(bank[2 + n % 2][:, b * P:(b + 1) * P],
                                                   prob[n % 4][:, b * P:(b + 1) * P], con(C_ID, P))
                    last.then_inc(ptp_done, 1)

                def times_v(n):
                    i, h, is_mem, blocks = unit(n)
                    pe.wait_ge(pt_ready[n % 2], l * (UNITS // 2) + (n // 2 + 1))
                    g = 2 * (TT - 1 - i) + is_mem
                    if h == 0 and g >= 2:
                        pe.wait_ge(y_ready, l * 2 * TT + (g - 1))
                    if h == 0 and g > pools_after and is_mem:
                        pe.wait_ge(ypool_lo, (l + 1) * 2)
                    if n == 0:
                        pe.wait_ge(mv_ready, (l + 1) * MT)
                    if g == 1 and h == 0:
                        pe.wait_ge(zn_ready, (l + 1) * NORMED)
                    p0, j = HD * (h % 2), h // 2
                    for b in range(blocks):
                        val = mv[:, b * MEM + h * HD:b * MEM + (h + 1) * HD] if is_mem else \
                            v[:, b * T + h * HD:b * T + (h + 1) * HD]
                        last = mm(y_bank(g)[p0:p0 + HD, j * P:(j + 1) * P], val,
                                  pt[n % 2][:, b * P:(b + 1) * P], b == 0, b == blocks - 1)
                    last.then_inc(pv_done, 1)

                def spread_sums(g):
                    pe.wait_ge(rinv_ready, l * 2 * TT + (g + 1))
                    if g >= 1:
                        pe.wait_ge(rt_ready, l * 2 * TT + g)
                    if g > pools_after:
                        pe.wait_ge(ypool_lo, l * 2 + 1)
                    for at_n in range(group_start(g), group_end(g)):
                        j, h = divmod(at_n - group_start(g), 2)
                        last = mm(bank[7][h * HD:(h + 1) * HD, j * P:(j + 1) * P],
                                  rinv[:, at_n:at_n + 1].broadcast_to([P, HD]), con(C_ID, P))
                    last.then_inc(rt_done, 1)

                for n in range(UNITS + LAG + 1):
                    if n in POOL_UNITS:
                        pool_map(POOL_UNITS.index(n))
                    if n < UNITS:
                        logits(n)
                    if NORM_EARLY + n < NORMED:
                        spread_rms(NORM_EARLY + n)
                    if n - 2 in group_after:
                        spread_sums(group_after[n - 2])
                    if 0 <= n - LAG < UNITS:
                        transpose_p(n - LAG)
                    if n in FILL:
                        fill(FILL[n])
                    if 0 <= n - LAG - 1 < UNITS:
                        times_v(n - LAG - 1)

                pe.wait_ge(yt_lo, l * 2 * TT + (2 * TT - 1))
                out_chunk(0, [5], len(FILL))
                out_chunk(1, [5], len(FILL))
                free = list(FILL.values()) + [5]
                out_chunk(2, free)
                pe.wait_ge(yt_lo, (l + 1) * 2 * TT)
                for k in range(3):
                    out_chunk(k, [6, 7], len(free))
                for k in range(3, DC):
                    out_chunk(k)

            pe.sem_inc(slot_done, RING)
            with pe.Fori(0, LAYERS) as l:
                ffn(l, 0)
                mix(l)
                ffn(l, 1)

        @block.scalar
        def _(act):
            def prepare(l, ph, gain, last_slot):
                for j in range(DC):
                    act.wait_ge(x_new, (l * 3 + ph) * DC + (j + 1))
                    nc.scalar.activation(chunk(h_hi, j), chunk(x, j), ACT.Copy,
                                         scale=par[:, ds(l * PARAMS + (gain + j), 1)])\
                        .then_inc(hi_ready, 1)
                    if ph == 0 and j == 3:
                        round_ahead(l, 1 - RING)
                for half in range(2):
                    s = slice(half * 4 * T, (half + 1) * 4 * T)
                    nc.scalar.activation(sq[:, s], x[:, s], ACT.Square).then_inc(sq_ready, 1)
                if ph == 0:
                    for n in range(2 - RING, -1):
                        round_ahead(l, n)
                round_ahead(l, last_slot)

            def root(l, ph):
                act.wait_ge(consts_loaded, 16)
                act.wait_ge(sum_done, l * 3 + (ph + 1))
                nc.scalar.activation(r[:, :], bank[4][:, :], ACT.Sqrt, bias=con(C_EPS),
                                     scale=1.0 / D).then_inc(rms_ready, 1)

            def round_ahead(l, n, off=0):
                pos = (n + RING) % RING
                s = slice(pos * SLOT, (pos + 1) * SLOT)
                act.wait_ge(slot_done, l * SLOTS + off + (n + RING + 1))
                act.wait_ge(w_loaded[pos], 16 * (SLOTS // RING) * l + off * (16 // RING)
                            + 16 * ((n + RING) // RING + 1))
                nc.scalar.activation(w_hi[:, s], raw[:, s], ACT.Copy).then_inc(w_hi_done, 1)

            def ffn(l, e):
                at = FFN_BASE[e]
                prepare(l, 2 * e, (G_FFN1, G_FFN2)[e], at - 1)
                root(l, 2 * e)
                with act.Fori(0, FC // 2) as i:
                    f = i * 2
                    for half in range(2):
                        done = (l * 2 + e) * FC + f + (half + 1)
                        g = chunk(t1, half)
                        round_ahead(l, at + 2 * half, f * 2)
                        act.wait_ge(gate_ready, done)
                        nc.scalar.activation(g, g, ACT.Silu).then_inc(silu_ready, 1)
                        round_ahead(l, at + 2 * half + 1, f * 2)
                        act.wait_ge(prod_ready, done)
                        nc.scalar.activation(a_hi[:, ds(f * T + half * T, T)], chunk(t2, half),
                                             ACT.Copy).then_inc(a_hi_ready, 1)
                down = at + 2 * FC
                rounds = (FC - RING) // RING
                with act.Fori(0, rounds) as i:
                    for off in range(RING):
                        round_ahead(l, down + off, i * RING)
                for n in range(rounds * RING, FC - 1 if e == 0 else FC - RING + 1):
                    round_ahead(l, down + n)

            def mix(l):
                prepare(l, 1, G_MIX, MIX_BASE["iq"] - 1)
                round_ahead(l, MIX_BASE["iq"])
                act.dma_start(mem[:, :], mem_t[:, :]).then_inc(mem_loaded, 16)
                act.dma_start(wpool[:, :], pool_w[ds(l, 1), :, :].rearrange("a p n -> (a p) n"))\
                    .then_inc(pool_w_loaded, 16)
                act.dma_start(spread_in[:, :], spreads[:, :]).then_inc(spread_loaded, 16)
                round_ahead(l, MIX_BASE["iq"] + 1)
                root(l, 1)
                act.wait_ge(mem_loaded, (l + 1) * 16)
                for j in range(DC):
                    s = slice(j * MEM, (j + 1) * MEM)
                    nc.scalar.activation(m_hi[:, s], mem[:, s], ACT.Copy,
                                         scale=par[:, ds(l * PARAMS + (G_MEM + j), 1)])\
                        .then_inc(m_hi_ready, 1)
                round_ahead(l, MIX_BASE["ik"])
                nc.scalar.activation(sq[:, 0:DC * MEM], mem[:, :], ACT.Square).then_inc(msq_ready, 1)
                for j in range(3):
                    act.wait_ge(proj_ready, l * 17 + (j + 1))
                    nc.scalar.activation(chunk(idx_hi, j), chunk(idx, j), ACT.Copy)\
                        .then_inc(idx_hi_ready, 1)
                round_ahead(l, MIX_BASE["iw"])
                round_ahead(l, MIX_BASE["av"])
                round_ahead(l, MIX_BASE["av"] + 1)
                n = 0
                for i in range(1, TT):
                    for h in range(IDX_HEADS):
                        act.wait_ge(dots_done, l * 12 + (n + 1))
                        if n >= 2:
                            act.wait_ge(acc_score, l * 12 + (n - 1))
                        nc.scalar.activation(chunk(t2, n % 2, T, (i + 1) * P), bank[n % 2][:, 0:(i + 1) * P],
                                             ACT.Relu, scale=HD ** -0.5 * IDX_HEADS ** -0.5)\
                            .then_inc(relu_ready, 1)
                        n += 1
                act.wait_ge(spread_loaded, (l + 1) * 16)
                nc.scalar.activation(spread[:, :], spread_in[:, :], ACT.Copy).then_inc(spread_ready, 1)
                round_ahead(l, MIX_BASE["av"] + 2)
                round_ahead(l, MIX_BASE["av"] + 3)
                act.wait_ge(msum_done, l + 1)
                nc.scalar.activation(rmem[:, :], bank[2][:, 0:MEM], ACT.Sqrt, bias=con(C_EPS),
                                     scale=1.0 / D).then_inc(mrms_ready, 1)
                act.wait_ge(cols_ready, l + 1)
                for i in range(TT):
                    nc.scalar.activation(chunk(v, i), bank[4 + i][:, :], ACT.Copy,
                                         scale=cols[:, i:i + 1]).then_inc(v_ready, 1)

                def squares(j):
                    act.wait_ge(proj_ready, l * 17 + (5 + j if j < ZT else 17))
                    if j >= 2:
                        act.wait_ge(zsum_done, l * (ZT + 1) + (j - 1))
                    src = mk[:, :] if ORDER[j] == "mk" else chunk(z, ORDER[j])
                    nc.scalar.activation(chunk(t1, j % 2), src, ACT.Square).then_inc(zsq_ready, 1)

                def split_hi(k):
                    j = NORM_ORDER[k]
                    act.wait_ge(zn_ready, l * NORMED + (k + 1))
                    t = chunk(z, j) if j < ZT else chunk(mk, j - ZT, MEM)
                    nc.scalar.activation(zn_hi[j], t, ACT.Copy).then_inc(zhi_ready, 1)

                def head_root(stage):
                    rows, n = head_rms(stage * ZT)
                    act.wait_ge(zsum_done, l * (ZT + 1) + (ZT + stage))
                    nc.scalar.activation(hrms[rows, 0:n], bank[6][rows, 0:n], ACT.Sqrt,
                                         bias=const[rows, C_EPS:C_EPS + 1],
                                         scale=1.0 / HD).then_inc(hrms_ready, 1)

                def head_hi(stage):
                    rows, n = head_rms(stage * ZT)
                    act.wait_ge(hinv_ready, l * 2 + (stage + 1))
                    nc.scalar.activation(hr_hi[rows, 0:n], hrms[rows, 0:n], ACT.Copy)\
                        .then_inc(hr_hi_ready, 1)

                for j in range(ZT):
                    round_ahead(l, MIX_BASE["aq"] + j)
                    squares(j)
                round_ahead(l, MIX_BASE["pu"])
                head_root(0)
                head_hi(0)
                round_ahead(l, MIX_BASE["pu"] + 1)
                for k in range(5):
                    split_hi(k)
                squares(ZT)
                for k in range(5, NORM_EARLY):
                    split_hi(k)
                head_root(1)
                act.wait_ge(slot_done, l * SLOTS + (RING + MIX_BASE["mv"] + 2))
                act.wait_ge(mcols_ready, l + 1)
                for i in range(MT):
                    nc.scalar.activation(chunk(mv, i, MEM), chunk(bank[5], i, MEM), ACT.Copy,
                                         scale=rmem_col[:, i:i + 1]).then_inc(mv_ready, 1)
                head_hi(1)

                def pool_hi(i):
                    act.wait_ge(pool_done, l * 2 + (i + 1))
                    nc.scalar.activation(chunk(y_hi, 4 + i), bank[7 - i][:, :], ACT.Copy,
                                         scale=par[:, ds(l * PARAMS + (G_POOL + i), 1)])\
                        .then_inc(ypool_hi, 1)

                def act_copy(to, src):
                    return nc.scalar.activation(to, src, ACT.Copy)

                def exps(n):
                    i, h, is_mem, blocks = unit(n)
                    act.wait_ge(lm_ready, l * UNITS + (n + 1))
                    if n >= 4:
                        act.wait_ge(ptp_done, l * UNITS + (n - 3))
                    nc.scalar.activation(prob[n % 4][:, 0:blocks * P], chunk(t2, n % 2, T, blocks * P),
                                         ACT.Exp, bias=negmax[:, n:n + 1], scale=-1.0,
                                         accum_out=rowsum[:, n:n + 1]).then_inc(p_ready, 1)

                def copy_rt(g):
                    act.wait_ge(rt_done, l * 2 * TT + (g + 1))
                    if g >= 1:
                        act.wait_ge(y_ready, l * 2 * TT + g)
                    c = (group_end(g) - group_start(g)) // 2 * P
                    nc.scalar.activation(rt[:, 0:c], bank[7][:, 0:c], ACT.Copy).then_inc(rt_ready, 1)

                def split_y(g):
                    i, is_mem = query_tile(g), g % 2
                    n = 2 if is_mem else 4
                    y = y_hi[:, (6 if is_mem else 0) * T:(8 if is_mem else 4) * T]
                    act.wait_ge(y_ready, l * 2 * TT + (g + 1))
                    nc.scalar.activation(y.rearrange("p (c t) -> p c t", t=T)[:, :, i * P:(i + 1) * P],
                                         yt[:, 0:n * P].rearrange("p (c t) -> p c t", t=P),
                                         ACT.Copy).then_inc(yt_hi, 1)

                for n in range(UNITS + LAG + 2):
                    if 0 <= n - LAG < UNITS and not on_vector(n - LAG):
                        copy_pt(act, act_copy, l, n - LAG)
                    if n < UNITS:
                        exps(n)
                    if NORM_EARLY + n < NORMED:
                        split_hi(NORM_EARLY + n)
                    if n in OUT_ROUND_UNITS:
                        round_ahead(l, MIX_BASE["out"] - RING + OUT_ROUND_UNITS.index(n))
                    if n - 1 in POOL_UNITS:
                        pool_hi(POOL_UNITS.index(n - 1))
                    if n - 2 in group_after:
                        copy_rt(group_after[n - 2])
                    if n - LAG - 1 in group_after:
                        split_y(group_after[n - LAG - 1])
                for k in range(DC - 1):
                    round_ahead(l, MIX_BASE["out"] + k)

            act.wait_ge(params_loaded, 16)
            round_ahead(0, -RING)
            with act.Fori(0, LAYERS) as l:
                ffn(l, 0)
                mix(l)
                ffn(l, 1)

        @block.vector
        def _(dve):
            V = nc.vector
            links = [0]

            def link(l, ins):
                links[0] += 1
                ins.then_inc(dve_chain, 1)
                dve.wait_ge(dve_chain, l * DVE_CHAIN + links[0])

            def prepare(l, ph, gain):
                for j in range(DC):
                    dve.wait_ge(hi_ready, (l * 3 + ph) * DC + (j + 1))
                    V.scalar_tensor_tensor(out=chunk(h_lo, j), in0=chunk(x, j),
                                           scalar=par[:, ds(l * PARAMS + (gain + j), 1)],
                                           in1=chunk(h_hi, j).bitcast(f32), op0=ALU.mult,
                                           op1=ALU.subtract).then_inc(lo_ready, 1)
                dve.wait_ge(sq_ready, (l * 3 + ph) * 2 + 2)
                for half in (4 * T, 2 * T):
                    link(l, V.tensor_tensor(out=sq[:, 0:half], in0=sq[:, 0:half],
                                            in1=sq[:, half:2 * half], op=ALU.add))
                V.tensor_tensor(out=sq[:, 0:T], in0=sq[:, 0:T], in1=sq[:, T:2 * T],
                                op=ALU.add).then_inc(ssq_ready, 1)

            def invert(l, ph):
                dve.wait_ge(rms_ready, l * 3 + (ph + 1))
                V.reciprocal(r[:, :], r[:, :]).then_inc(r_ready, 1)
                wait_apart(dve, r_ready, l * 3 + (ph + 1))

            def update(l, ph, acc_at, slot_at, scale):
                for j in range(DC):
                    if j < ACC:
                        dve.wait_ge(acc_done, l * ACC_LAYER + (acc_at + j + 1))
                    else:
                        dve.wait_ge(slot_done, l * SLOTS + (RING + slot_at))
                    V.scalar_tensor_tensor(out=chunk(x, j), in0=bank[j][:, :], scalar=scale,
                                           in1=chunk(x, j), op0=ALU.mult, op1=ALU.add)\
                        .then_inc(x_new, 1)

            def ffn(l, e):
                ph = 2 * e
                prepare(l, ph, (G_FFN1, G_FFN2)[e])
                invert(l, ph)
                with dve.Fori(0, FC // 2) as i:
                    f = i * 2
                    for half in range(2):
                        done = (l * 2 + e) * FC + f + (half + 1)
                        slot = l * SLOTS + f * 2 + (RING + FFN_BASE[e] + 2 * half)
                        g, h = chunk(t1, half), chunk(t2, half)
                        dve.wait_ge(slot_done, slot + 1)
                        V.tensor_tensor(out=g, in0=bank[2 * half][:, :], in1=r[:, :],
                                        op=ALU.mult).then_inc(gate_ready, 1)
                        dve.wait_ge(slot_done, slot + 2)
                        V.tensor_tensor(out=h, in0=bank[2 * half + 1][:, :], in1=r[:, :],
                                        op=ALU.mult).then_inc(gu_free, 1)
                        dve.wait_ge(gu_free, done + 2)
                        dve.wait_ge(silu_ready, done)
                        V.tensor_tensor(out=h, in0=g, in1=h, op=ALU.mult).then_inc(prod_ready, 1)
                        dve.wait_ge(a_hi_ready, done)
                        V.tensor_tensor(out=a_lo[:, ds(f * T + half * T, T)], in0=h,
                                        in1=a_hi[:, ds(f * T + half * T, T)].bitcast(f32),
                                        op=ALU.subtract).then_inc(a_lo_ready, 1)
                update(l, ph, ACC_BASE[2 * e] + ACC * (FC - 1), FFN_BASE[e] + FFN_SLOTS, 0.5)

            def mix(l):
                prepare(l, 1, G_MIX)
                invert(l, 1)

                def evacuate(j, slot, out_, in_, rr):
                    dve.wait_ge(slot_done, l * SLOTS + (RING + slot + 1))
                    V.tensor_tensor(out=out_, in0=in_, in1=rr, op=ALU.mult).then_inc(proj_ready, 1)

                for j in range(3):
                    evacuate(j, MIX_BASE["iq"] + j, chunk(idx, j), bank[j][:, :], r[:, :])
                dve.wait_ge(msq_ready, l + 1)
                for half in (4 * MEM, 2 * MEM):
                    link(l, V.tensor_tensor(out=sq[:, 0:half], in0=sq[:, 0:half],
                                            in1=sq[:, half:2 * half], op=ALU.add))
                V.tensor_tensor(out=sq[:, 0:MEM], in0=sq[:, 0:MEM], in1=sq[:, MEM:2 * MEM],
                                op=ALU.add).then_inc(mssq_ready, 1)
                dve.wait_ge(m_hi_ready, (l + 1) * DC)
                for j in range(DC):
                    s = slice(j * MEM, (j + 1) * MEM)
                    last = V.scalar_tensor_tensor(out=m_lo[:, s], in0=mem[:, s],
                                                  scalar=par[:, ds(l * PARAMS + (G_MEM + j), 1)],
                                                  in1=m_hi[:, s].bitcast(f32), op0=ALU.mult,
                                                  op1=ALU.subtract)
                last.then_inc(m_lo_ready, 1)
                for j in range(3):
                    dve.wait_ge(idx_hi_ready, l * 3 + (j + 1))
                    V.tensor_tensor(out=chunk(idx_lo, j), in0=chunk(idx, j),
                                    in1=chunk(idx_hi, j).bitcast(f32),
                                    op=ALU.subtract).then_inc(idx_lo_ready, 1)
                evacuate(3, MIX_BASE["iw"], iw[0:4, :], bank[3][0:4, :], r[0:4, :])
                dve.wait_ge(cols_done, l + 1)
                V.tensor_copy(cols[:, :], bank[3][:, 0:TT + 4 * TT]).then_inc(cols_ready, 1)
                dve.wait_ge(cols_ready, l + 1)

                n = 0
                for i in range(1, TT):
                    s = score[:, score_at[i]:score_at[i] + (i + 1) * P]
                    for h in range(IDX_HEADS):
                        dve.wait_ge(relu_ready, l * 12 + (n + 1))
                        c = TT + 4 * i + h
                        before = con(C_CAUSAL + T - (i + 1) * P, (i + 1) * P) if h == 0 else s
                        V.scalar_tensor_tensor(out=s, in0=chunk(t2, n % 2, T, (i + 1) * P),
                                               scalar=cols[:, c:c + 1], in1=before, op0=ALU.mult,
                                               op1=ALU.add).then_inc(acc_score, 1)
                        n += 1
                        wait_apart(dve, acc_score, l * 12 + n)

                def take_largest(before):
                    tiles = [(score[:, score_at[i]:score_at[i] + (i + 1) * P],
                              top8[:, 8 * i:8 * (i + 1)]) for i in range(TT - 1, 0, -1)]
                    for k, (s, top) in enumerate(tiles):
                        wait_apart(dve, dve_chain, before + (k - len(tiles) + 1))
                        V.max(top, s).then_inc(dve_chain, 1)
                    for k, (s, top) in enumerate(tiles):
                        wait_apart(dve, dve_chain, before + (k + 1))
                        V.match_replace(s, top, s, TAKEN).then_inc(dve_chain, 1)

                with dve.Fori(0, FIRST_ROUNDS) as q:
                    take_largest(l * DVE_CHAIN + q * ROUND_CHAIN + links[0])
                links[0] += ROUND_CHAIN * FIRST_ROUNDS
                dve.wait_ge(mrms_ready, l + 1)
                V.reciprocal(rmem[:, :], rmem[:, :]).then_inc(rmem_ready, 1)
                for j in range(ZT):
                    tile = ORDER[j]
                    name, i = ("aq", "ak", "mq")[tile // 4], tile % 4
                    evacuate(4 + j, MIX_BASE[name] + i, chunk(z, tile), bank[tile % 4][:, :],
                             r[:, :])
                    take_largest(l * DVE_CHAIN + links[0])
                    links[0] += ROUND_CHAIN
                dve.wait_ge(mcols_done, l + 1)
                V.tensor_copy(rmem_col[:, :], bank[7][:, 0:MT]).then_inc(mcols_ready, 1)
                evacuate(14, MIX_BASE["pu"], chunk(u, 0), bank[2][:, :], r[:, :])

                def head_inverse(stage):
                    rows, n = head_rms(stage * ZT)
                    dve.wait_ge(hrms_ready, l * 2 + (stage + 1))
                    V.reciprocal(hrms[rows, 0:n], hrms[rows, 0:n]).then_inc(hinv_ready, 1)

                def head_lo(stage):
                    rows, n = head_rms(stage * ZT)
                    dve.wait_ge(hr_hi_ready, l * 2 + (stage + 1))
                    V.tensor_tensor(out=hr_lo[rows, 0:n], in0=hrms[rows, 0:n],
                                    in1=hr_hi[rows, 0:n].bitcast(f32),
                                    op=ALU.subtract).then_inc(hr_lo_ready, 1)

                def normalise(k):
                    j = NORM_ORDER[k]
                    gain = ([G_Q] * 4 + [G_K] * 4 + [G_MQ] * 2 + [G_MK] * 2)[j]
                    dve.wait_ge(spread_done, l * NORMED + (k + 1))
                    t = chunk(z, j) if j < ZT else chunk(mk, j - ZT, MEM)
                    V.scalar_tensor_tensor(out=t, in0=t, scalar=par[:, ds(l * PARAMS + gain, 1)],
                                           in1=spread_bank(k)[:, 0:head_rms(j)[1]], op0=ALU.mult,
                                           op1=ALU.mult).then_inc(zn_ready, 1)

                head_inverse(0)
                dve.wait_ge(dve_chain, l * DVE_CHAIN + links[0])
                V.tensor_scalar(score[:, :], score[:, :], TAKEN, NEG, ALU.not_equal,
                                ALU.mult).then_inc(bias_ready, 1)
                head_lo(0)
                evacuate(15, MIX_BASE["pu"] + 1, chunk(u, 1), bank[3][:, :], r[:, :])
                for k in range(5):
                    normalise(k)
                dve.wait_ge(slot_done, l * SLOTS + (RING + MIX_BASE["mk"] + 2))
                dve.wait_ge(rmem_ready, l + 1)
                for i in range(2):
                    last = V.tensor_tensor(out=chunk(mk, i, MEM), in0=chunk(bank[4], i, MEM),
                                           in1=rmem[:, :], op=ALU.mult)
                last.then_inc(proj_ready, 1)
                for k in range(5, NORM_EARLY):
                    normalise(k)
                head_inverse(1)
                head_lo(1)
                dve.wait_ge(bias_ready, l + 1)

                def pool_lo(i):
                    dve.wait_ge(ypool_hi, l * 2 + (i + 1))
                    V.scalar_tensor_tensor(out=chunk(y_lo, 4 + i), in0=bank[7 - i][:, :],
                                           scalar=par[:, ds(l * PARAMS + (G_POOL + i), 1)],
                                           in1=chunk(y_hi, 4 + i).bitcast(f32), op0=ALU.mult,
                                           op1=ALU.subtract).then_inc(ypool_lo, 1)

                def mask_and_max(n):
                    i, h, is_mem, blocks = unit(n)
                    if is_mem:
                        bias = con(C_CAUSAL, MEM)
                    elif i == 0:
                        bias = con(C_CAUSAL + T - P, P)
                    else:
                        bias = score[:, score_at[i]:score_at[i] + blocks * P]
                    if n >= 2:
                        dve.wait_ge(p_ready, l * UNITS + (n - 1))
                    wait_apart(dve, logit_done, l * UNITS + (n + 1))
                    V.tensor_tensor_reduce(out=chunk(t2, n % 2, T, blocks * P),
                                           in0=logit_bank[n % 3][:, 0:blocks * P], in1=bias,
                                           scale=-HD ** -0.5, scalar=-TAKEN, op0=ALU.add, op1=ALU.min,
                                           accum_out=negmax[:, n:n + 1]).then_inc(lm_ready, 1)

                def invert_sums(g):
                    units = slice(group_start(g), group_end(g))
                    dve.wait_ge(p_ready, l * UNITS + group_end(g))
                    V.reciprocal(rinv[:, units], rowsum[:, units]).then_inc(rinv_ready, 1)

                def over_sums(g):
                    dve.wait_ge(pv_done, l * UNITS + group_end(g))
                    dve.wait_ge(rt_ready, l * 2 * TT + (g + 1))
                    if g >= 1:
                        dve.wait_ge(yt_lo, l * 2 * TT + g)
                    c = (group_end(g) - group_start(g)) // 2 * P
                    V.tensor_tensor(out=yt[:, 0:c], in0=y_bank(g)[:, 0:c], in1=rt[:, 0:c],
                                    op=ALU.mult).then_inc(y_ready, 1)

                def split_y(g):
                    i, is_mem = query_tile(g), g % 2
                    n = 2 if is_mem else 4
                    lo, hi = (t[:, (6 if is_mem else 0) * T:(8 if is_mem else 4) * T]
                              .rearrange("p (c t) -> p c t", t=T)[:, :, i * P:(i + 1) * P]
                              for t in (y_lo, y_hi))
                    dve.wait_ge(yt_hi, l * 2 * TT + (g + 1))
                    V.tensor_tensor(out=lo, in0=yt[:, 0:n * P].rearrange("p (c t) -> p c t", t=P),
                                    in1=hi.bitcast(f32), op=ALU.subtract).then_inc(yt_lo, 1)

                for n in range(UNITS + LAG + 3):
                    if n < UNITS:
                        mask_and_max(n)
                    if 0 <= n - LAG < UNITS and on_vector(n - LAG):
                        copy_pt(dve, V.tensor_copy, l, n - LAG)
                    if n in group_after:
                        invert_sums(group_after[n])
                    if n - LAG - 1 in group_after:
                        over_sums(group_after[n - LAG - 1])
                    if NORM_EARLY + n < NORMED:
                        normalise(NORM_EARLY + n)
                    if n - 1 in POOL_UNITS:
                        pool_lo(POOL_UNITS.index(n - 1))
                    if n - LAG - 2 in group_after:
                        split_y(group_after[n - LAG - 2])
                update(l, 1, ACC_BASE[1] + ACC * (DC - 1), MIX_BASE["out"] + DC, 1.0)

            dve.wait_ge(params_loaded, 16)
            for q in range(X_PARTS):
                dve.wait_ge(x_loaded[q], 16)
                dve.sem_inc(x_new, DC // X_PARTS)
            dve.sem_inc(gu_free, 2)
            with dve.Fori(0, LAYERS) as l:
                ffn(l, 0)
                mix(l)
                ffn(l, 1)
            assert links[0] == DVE_CHAIN, links[0]


def _constants():
    import numpy as np

    c = np.zeros((P, CONSTS), np.float32)
    p = np.arange(P)
    c[:, C_ID:C_ID + P] = np.eye(P)
    c[:, C_ONES:C_ONES + P] = 1
    c[:, C_CAUSAL + T - P:C_CAUSAL + T] = np.where(p[None, :] <= p[:, None], 0, NEG)
    for half in range(2):
        for j in range(ZT):
            c[half * HD:(half + 1) * HD, C_SEL + j * Z_ROWS + 2 * j + half] = 1
        for i in range(NORMED - ZT):
            c[half * HD:(half + 1) * HD, C_SEL_MK + i * MK_ROWS + 2 * i + half] = 1
    for i in range(2):
        for half in range(2):
            w = WINDOWS[2 * i + half]
            s = slice(half * HD, (half + 1) * HD)
            c[s, C_INV + 16 * i:C_INV + 16 * (i + 1)] = 1 / np.minimum(np.arange(16) + 1, w)
            c[s, C_INVW + i] = 1 / w
    c[:, C_EPS] = EPS
    return c


def _spread():
    import numpy as np

    c = np.zeros((NROW, NORMED * P), np.float32)
    for head in range(2 * NORMED):
        row = head if head < Z_ROWS else MK_ROW + head - Z_ROWS
        c[row, head * HD:(head + 1) * HD] = 1
    return c


def _by_output(w, n):
    return w.reshape(DC, P, n, P).transpose(2, 1, 0, 3).reshape(n, P, SLOT)


def _weight_stream(a, l):
    import numpy as np

    def ffn(gate, up, down):
        gu = np.stack([_by_output(gate, FC), _by_output(up, FC)], 1).reshape(2 * FC, P, SLOT)
        return [gu, down.reshape(FC, P, SLOT)]

    def by_tokens(w, chunks):
        return w.reshape(DC // chunks, chunks, P, -1).transpose(0, 2, 1, 3).reshape(-1, P, SLOT)

    w = a["w_in"][l]
    at = np.cumsum([0, 512, 512, 512, 256, 64, 4, 256, 256])
    aq, ak, av, iq, ik, iw, pu, mq = (w[:, at[i]:at[i + 1]] for i in range(8))
    kv = a["w_mem_kv"][l]
    iw = np.concatenate([iw, np.zeros((D, P - 4), iw.dtype)], 1)
    parts = ffn(a["ffn1_gate"][l], a["ffn1_up"][l], a["ffn1_down"][l])
    parts += [_by_output(iq, 2), _by_output(np.concatenate([ik, ik], 1), 1), _by_output(iw, 1),
              by_tokens(av, 2), _by_output(aq, 4), _by_output(ak, 4), _by_output(mq, 2),
              _by_output(pu, 2), _by_output(kv[:, :256], 2), by_tokens(kv[:, 256:], 4),
              a["w_out"][l].reshape(DC, P, SLOT)[OUT_ORDER]]
    parts += ffn(a["ffn2_gate"][l], a["ffn2_up"][l], a["ffn2_down"][l])
    return parts


def kernel(**inputs):
    import numpy as np
    import concourse.bacc as bacc
    from concourse.bass_utils import run_bass_kernel_spmd

    a = {k: np.asarray(v) for k, v in inputs.items()}

    def transposed(m):
        return m.reshape(-1, DC, P).transpose(2, 1, 0).reshape(P, -1)

    params = []
    pool_w = np.zeros((LAYERS, P, 2 * P), np.float32)
    for l in range(LAYERS):
        for name in ("ffn1_norm", "mix_norm", "ffn2_norm", "mem_norm"):
            params.append(a[name][l].reshape(DC, P).T)
        for name in ("q_norm", "k_norm", "mq_norm", "mk_norm"):
            params.append(np.concatenate([a[name][l]] * 2)[:, None])
        params.append(a["pool_scale"][l].reshape(2, P).T)
        for g in range(4):
            i, half = divmod(g, 2)
            pool_w[l, half * HD:(half + 1) * HD, i * P + half * HD:i * P + (half + 1) * HD] = a["w_pool"][l, g]
    data = {
        "x_t": transposed(a["x"][0]),
        "mem_t": transposed(a["mem"][0]),
        "weights": np.concatenate([p for l in range(LAYERS) for p in _weight_stream(a, l)]
                                  + [np.zeros((RING, P, SLOT), np.float32)], 0),
        "pool_w": pool_w,
        "params": np.concatenate(params, 1),
        "consts": _constants(),
        "spreads": _spread(),
    }
    nc = bacc.Bacc("TRN2", target_bir_lowering=False, num_devices=1)
    arrays, args = {}, []
    for name, v in data.items():
        arrays[name] = np.ascontiguousarray(v)
        args.append(nc.dram_tensor(name, arrays[name].shape, mybir.dt.from_np(arrays[name].dtype),
                                   kind="ExternalInput").ap())
    out = nc.dram_tensor("out_t", (P, DC * T), mybir.dt.float32, kind="ExternalOutput").ap()
    build(nc, *args, out)
    res = run_bass_kernel_spmd(nc, [arrays], core_ids=[0])
    got = res.results[0]["out_t"].reshape(P, DC, T).transpose(2, 1, 0).reshape(1, T, D)
    return np.ascontiguousarray(got)
```
